# Optimizing a Trainium2 kernel written in Bass

```python
import jax, jax.numpy as jnp
from jax import lax
import numpy as np
import math

D_MODEL = 1024
BATCH = 1
SEQ = 512
DEPTH = 2

N_MIXERS = 2
PLE_DIM = 256
ATT_HEADS = 16
ATT_HEAD_DIM = 64
ATT_WIDTH = ATT_HEADS * ATT_HEAD_DIM
QUERY_BLOCK = 128
REC_HEADS = 8
REC_KEY_DIM = 128
REC_VAL_DIM = 128
REC_WIDTH = REC_HEADS * REC_KEY_DIM
REC_VWIDTH = REC_HEADS * REC_VAL_DIM
CHUNK = 64
N_ATT_LAYERS = (DEPTH + 1) // 2
N_REC_LAYERS = DEPTH // 2
EPS = 1e-6


def rms_norm(x, gain):
    xf = x.astype(jnp.float32)
    y = xf * lax.rsqrt(jnp.mean(xf * xf, axis=-1, keepdims=True) + EPS)
    return (y * gain.astype(jnp.float32)).astype(x.dtype)

def fox_attention(q, k, v, c):
    B, H, S, hd = q.shape
    scale = hd ** -0.5
    kpos = jnp.arange(S)

    def block(i):
        start = i * QUERY_BLOCK
        qb = lax.dynamic_slice_in_dim(q, start, QUERY_BLOCK, axis=2)
        cb = lax.dynamic_slice_in_dim(c, start, QUERY_BLOCK, axis=2)
        s = jnp.einsum('bhqd,bhkd->bhqk', qb, k).astype(jnp.float32) * scale
        s = s + (cb[..., :, None] - c[..., None, :])
        qpos = start + jnp.arange(QUERY_BLOCK)
        s = jnp.where(kpos[None, :] <= qpos[:, None], s, -jnp.inf)
        w = jax.nn.softmax(s, axis=-1)
        return jnp.einsum('bhqk,bhkd->bhqd', w.astype(v.dtype), v)

    out = lax.map(block, jnp.arange(S // QUERY_BLOCK))
    return out.transpose(1, 0, 3, 2, 4).reshape(B, S, H * hd)

def fox_mixer(u, w_in, b_f, w_out):
    B, S, _ = u.shape
    proj = u @ w_in
    q, k, v, g, fl = jnp.split(proj, [ATT_WIDTH, 2 * ATT_WIDTH, 3 * ATT_WIDTH, 4 * ATT_WIDTH], axis=-1)
    heads = lambda t: t.reshape(B, S, ATT_HEADS, ATT_HEAD_DIM).transpose(0, 2, 1, 3)
    log_f = jax.nn.log_sigmoid(fl.astype(jnp.float32) + b_f.astype(jnp.float32))
    c = jnp.cumsum(log_f, axis=1).transpose(0, 2, 1)
    attn = fox_attention(heads(q), heads(k), heads(v), c)
    return (attn * jax.nn.silu(g)) @ w_out

def hgrn2_mixer(u, w_in, lb, out_gain, w_out):
    B, S, _ = u.shape
    proj = u @ w_in
    q, fl, inp, g = jnp.split(proj, [REC_WIDTH, 2 * REC_WIDTH, 2 * REC_WIDTH + REC_VWIDTH], axis=-1)
    lbf = lb.astype(jnp.float32)
    log_f = jnp.logaddexp(jnp.log(lbf), jnp.log1p(-lbf) + jax.nn.log_sigmoid(fl.astype(jnp.float32)))
    k = -jnp.expm1(log_f)

    def chunks(t, dh):
        return t.astype(jnp.float32).reshape(B, S // CHUNK, CHUNK, REC_HEADS, dh).transpose(1, 0, 3, 2, 4)

    qc, kc, gc = chunks(q, REC_KEY_DIM), chunks(k, REC_KEY_DIM), chunks(log_f, REC_KEY_DIM)
    ic = chunks(inp, REC_VAL_DIM)
    causal = jnp.tril(jnp.ones((CHUNK, CHUNK), dtype=bool))

    def step(state, xs):
        qb, kb, gb, ib = xs
        b = jnp.cumsum(gb, axis=-2)
        diff = b[..., :, None, :] - b[..., None, :, :]
        decay = jnp.exp(jnp.where(causal[:, :, None], diff, -jnp.inf))
        scores = jnp.einsum('bhtd,bhsd,bhtsd->bhts', qb, kb, decay)
        o = scores @ ib + jnp.einsum('bhtd,bhdv->bhtv', qb * jnp.exp(b), state)
        b_last = b[..., -1:, :]
        state = jnp.exp(b_last[..., 0, :])[..., None] * state + \
            jnp.einsum('bhsd,bhsv->bhdv', kb * jnp.exp(b_last - b), ib)
        return state, o

    state0 = jnp.zeros((B, REC_HEADS, REC_KEY_DIM, REC_VAL_DIM), jnp.float32)
    _, o = lax.scan(step, state0, (qc, kc, gc, ic))
    o = o.transpose(1, 0, 3, 2, 4).reshape(B, S, REC_HEADS, REC_VAL_DIM)
    o = o * lax.rsqrt(jnp.mean(o * o, axis=-1, keepdims=True) + EPS) * out_gain.astype(jnp.float32)
    gh = g.astype(jnp.float32).reshape(B, S, REC_HEADS, REC_VAL_DIM)
    y = (o * jax.nn.silu(gh)).reshape(B, S, REC_VWIDTH).astype(u.dtype)
    return y @ w_out

def first_inputs(seed: int = 0) -> dict:
    key = jax.random.key(seed)
    ks = jax.random.split(key, 14)
    nrm = jax.random.normal
    D = D_MODEL
    return {
        "x": nrm(ks[0], (BATCH, SEQ, D), jnp.float32),
        "p": nrm(ks[1], (DEPTH, BATCH, SEQ, PLE_DIM), jnp.float32),
        "norm_pre": 1.0 + 0.05 * nrm(ks[2], (DEPTH, D), jnp.float32),
        "norm_post": 1.0 + 0.05 * nrm(ks[3], (DEPTH, D), jnp.float32),
        "att_w_in": nrm(ks[4], (N_ATT_LAYERS, D, 4 * ATT_WIDTH + ATT_HEADS), jnp.float32) * D ** -0.5,
        "att_b_f": jax.random.uniform(ks[5], (N_ATT_LAYERS, ATT_HEADS), jnp.float32, 1.0, 6.0),
        "att_w_out": nrm(ks[6], (N_ATT_LAYERS, ATT_WIDTH, D), jnp.float32) * ATT_WIDTH ** -0.5,
        "rec_w_in": nrm(ks[7], (N_REC_LAYERS, D, 2 * REC_WIDTH + 2 * REC_VWIDTH), jnp.float32) * D ** -0.5,
        "rec_lb": 1.0 + 0.1 * nrm(ks[8], (DEPTH, REC_WIDTH), jnp.float32),
        "rec_out_norm": 1.0 + 0.05 * nrm(ks[9], (N_REC_LAYERS, REC_VAL_DIM), jnp.float32),
        "rec_w_out": nrm(ks[10], (N_REC_LAYERS, REC_VWIDTH, D), jnp.float32) * REC_VWIDTH ** -0.5,
        "ple_w_proj": nrm(ks[11], (DEPTH, PLE_DIM, D), jnp.float32) * PLE_DIM ** -0.5,
        "ple_w_gate": nrm(ks[12], (DEPTH, D, D), jnp.float32) * D ** -0.5,
    }

def first_block(x, p, norm_pre, norm_post, att_w_in, att_b_f, att_w_out, rec_w_in, rec_lb,
              rec_out_norm, rec_w_out, ple_w_proj, ple_w_gate):
    sm = jax.nn.softmax(rec_lb.astype(jnp.float32), axis=0)
    lower_bounds = jnp.cumsum(sm, axis=0) - sm[0:1]
    h = x
    for layer in range(DEPTH):
        u = rms_norm(h, norm_pre[layer])
        j = layer // N_MIXERS
        if layer % N_MIXERS == 0:
            y = fox_mixer(u, att_w_in[j], att_b_f[j], att_w_out[j])
        else:
            y = hgrn2_mixer(u, rec_w_in[j], lower_bounds[layer], rec_out_norm[j], rec_w_out[j])
        h = h + rms_norm(y, norm_post[layer])
        gate = jax.nn.sigmoid((h @ ple_w_gate[layer]).astype(jnp.float32)).astype(h.dtype)
        h = h + (p[layer] @ ple_w_proj[layer]) * gate
    return h


DEPTH_2 = 1

GRID_W = 64
F32 = jnp.float32
HY_WIDTH = D_MODEL // 4
NA_HEAD_DIM = 64
NA_WIDTH = D_MODEL // 2
NA_HEADS = NA_WIDTH // NA_HEAD_DIM
POOL_WIDTH = D_MODEL // 4
POOL_WINDOWS = (2, 4, 8, 16)
POOL_GROUPS = len(POOL_WINDOWS)
POOL_GROUP_DIM = POOL_WIDTH // POOL_GROUPS
IN_WIDTH = 3 * HY_WIDTH + 3 * NA_WIDTH + POOL_WIDTH
SHORT_CONV = 3
FILTER_EMB = 33
FILTER_BANDS = (FILTER_EMB - 1) // 2
FILTER_HIDDEN = 64
DECAY_FAST = 0.3
DECAY_SLOW = 1.5
DECAY_TARGET = 1e-2
NA_KH_MAX = 8
NA_KW = 16
N_EXPERTS = 16
EC_CAPACITY = 2
EXPERT_FF = 2 * D_MODEL


def rms_norm_2(x, g):
    xf = x.astype(F32)
    y = xf * lax.rsqrt(jnp.mean(xf * xf, axis=-1, keepdims=True) + EPS)
    return (y * g.astype(F32)).astype(x.dtype)

def short_conv(u, w, b):
    up = jnp.pad(u, ((0, 0), (1, 1), (0, 0)))
    return up[:, :-2] * w[0] + up[:, 1:-1] * w[1] + up[:, 2:] * w[2] + b

def hyena_filter(L, w1, b1, w2, b2, w_out, freq):
    t = jnp.linspace(0.0, 1.0, L, dtype=F32)[:, None]
    ang = 2.0 * math.pi * jnp.arange(L, dtype=F32)[:, None] / L
    f = jnp.linspace(1e-4, FILTER_BANDS - 1, FILTER_BANDS, dtype=F32)[None, :]
    z = jnp.concatenate([t, jnp.cos(f * ang), -jnp.sin(f * ang)], axis=-1)
    fr = freq.astype(F32)
    h = jnp.sin(fr * (z @ w1.astype(F32) + b1.astype(F32)))
    h = jnp.sin(fr * (h @ w2.astype(F32) + b2.astype(F32)))
    h = h @ w_out.astype(F32)
    deltas = jnp.abs(jnp.linspace(math.log(DECAY_TARGET) / DECAY_FAST,
                                  math.log(DECAY_TARGET) / DECAY_SLOW, HY_WIDTH, dtype=F32))
    decay = jnp.exp(-t * deltas)
    h = h * jnp.concatenate([decay, decay], axis=-1)
    h_fwd, h_bwd = h[:, :HY_WIDTH], h[:, HY_WIDTH:]
    return jnp.concatenate([h_fwd, jnp.zeros((1, HY_WIDTH), F32), h_bwd[1:][::-1]], axis=0)

def hyena_mixer(u, sw, sb, filt, skip):
    u = short_conv(u, sw, sb)
    x0, x1, v = jnp.split(u, 3, axis=-1)
    z = (v * x1).astype(F32)
    L = z.shape[1]
    Z = jnp.fft.rfft(z, n=2 * L, axis=1)
    Hf = jnp.fft.rfft(filt, n=2 * L, axis=0)
    y = jnp.fft.irfft(Z * Hf[None], n=2 * L, axis=1)[:, :L]
    y = y + z * skip.astype(F32)
    return y.astype(u.dtype) * x0

def neighbourhood_attention(q, k, v, rpb):
    B, L, _ = q.shape
    rows = L // GRID_W
    kh = min(NA_KH_MAX, rows)
    shp = (B, rows, GRID_W, NA_HEADS, NA_HEAD_DIM)
    qg = (q * (NA_HEAD_DIM ** -0.5)).reshape(shp).transpose(1, 0, 2, 3, 4)
    kg = k.reshape(shp)
    vg = v.reshape(shp)
    cols = jnp.arange(GRID_W)
    col_start = jnp.clip(cols - NA_KW // 2, 0, GRID_W - NA_KW)
    col_idx = col_start[:, None] + jnp.arange(NA_KW)[None, :]
    dc_idx = col_idx - cols[:, None] + NA_KW - 1

    def one_row(args):
        q_row, r = args
        rs = jnp.clip(r - kh // 2, 0, rows - kh)
        k_nb = lax.dynamic_slice_in_dim(kg, rs, kh, axis=1)[:, :, col_idx]
        v_nb = lax.dynamic_slice_in_dim(vg, rs, kh, axis=1)[:, :, col_idx]
        s = jnp.einsum('bchd,bicjhd->bhcij', q_row, k_nb).astype(F32)
        dr_idx = rs + jnp.arange(kh) - r + NA_KH_MAX - 1
        bias = rpb[:, dr_idx][:, :, dc_idx].transpose(0, 2, 1, 3)
        s = s + bias.astype(F32)[None]
        p = jax.nn.softmax(s.reshape(B, NA_HEADS, GRID_W, kh * NA_KW), axis=-1)
        p = p.reshape(s.shape).astype(v_nb.dtype)
        return jnp.einsum('bhcij,bicjhd->bchd', p, v_nb)

    out = lax.map(one_row, (qg, jnp.arange(rows)))
    return out.transpose(1, 0, 2, 3, 4).reshape(B, L, NA_WIDTH)

def pool_mixer(u, pool_w, pool_scale):
    B, L, _ = u.shape
    ug = u.reshape(B, L, POOL_GROUPS, POOL_GROUP_DIM).astype(F32)
    S = jnp.concatenate([jnp.zeros((B, 1, POOL_GROUPS, POOL_GROUP_DIM), F32),
                         jnp.cumsum(ug, axis=1)], axis=1)
    t = jnp.arange(L)
    means = []
    for g, w in enumerate(POOL_WINDOWS):
        lo = jnp.clip(t - w // 2, 0, L)
        hi = jnp.clip(t + w // 2, 0, L)
        cnt = (hi - lo).astype(F32)[None, :, None]
        means.append((S[:, hi, g] - S[:, lo, g]) / cnt)
    pooled = jnp.stack(means, axis=2) - ug
    y = jnp.einsum('blgc,gcd->blgd', pooled, pool_w.astype(F32)).reshape(B, L, POOL_WIDTH)
    return (y * pool_scale.astype(F32)).astype(u.dtype)

def expert_choice_moe(h, w_router, w_gate, w_up, w_down):
    B, L, D = h.shape
    cap = EC_CAPACITY * L // N_EXPERTS
    aff = jax.nn.softmax(h.astype(F32) @ w_router.astype(F32), axis=-1)
    gate, idx = lax.top_k(aff.transpose(0, 2, 1), cap)
    xs = jax.vmap(lambda hb, ib: hb[ib])(h, idx)
    a = jnp.einsum('becd,edf->becf', xs, w_gate)
    b = jnp.einsum('becd,edf->becf', xs, w_up)
    y = jnp.einsum('becf,efd->becd', jax.nn.silu(a) * b, w_down)
    y = y * gate.astype(y.dtype)[..., None]
    return jax.vmap(lambda yb, ib: jnp.zeros((L, D), yb.dtype).at[ib.reshape(-1)].add(
        yb.reshape(-1, D)))(y, idx)

def second_inputs(seed: int = 0) -> dict:
    key = jax.random.key(seed)
    ks = jax.random.split(key, 24)
    n = lambda k, s, sc: jax.random.normal(k, s, F32) * sc
    gain = lambda k, s: 1.0 + 0.02 * jax.random.normal(k, s, F32)
    L_ = DEPTH_2
    return {
        'x': jax.random.normal(ks[0], (BATCH, SEQ, D_MODEL), F32),
        'norm1_g': gain(ks[1], (L_, D_MODEL)),
        'w_in': n(ks[2], (L_, D_MODEL, IN_WIDTH), D_MODEL ** -0.5),
        'hy_short_w': n(ks[3], (L_, SHORT_CONV, 3 * HY_WIDTH), SHORT_CONV ** -0.5),
        'hy_short_b': n(ks[4], (L_, 3 * HY_WIDTH), 0.02),
        'hy_f_w1': n(ks[5], (L_, FILTER_EMB, FILTER_HIDDEN), FILTER_EMB ** -0.5),
        'hy_f_b1': n(ks[6], (L_, FILTER_HIDDEN), 0.02),
        'hy_f_w2': n(ks[7], (L_, FILTER_HIDDEN, FILTER_HIDDEN), FILTER_HIDDEN ** -0.5),
        'hy_f_b2': n(ks[8], (L_, FILTER_HIDDEN), 0.02),
        'hy_f_wout': n(ks[9], (L_, FILTER_HIDDEN, 2 * HY_WIDTH), FILTER_HIDDEN ** -0.5),
        'hy_f_freq': gain(ks[10], (L_, FILTER_HIDDEN)),
        'hy_skip': n(ks[11], (L_, HY_WIDTH), 1.0),
        'na_rpb': n(ks[12], (L_, NA_HEADS, 2 * NA_KH_MAX - 1, 2 * NA_KW - 1), 0.02),
        'pool_w': n(ks[13], (L_, POOL_GROUPS, POOL_GROUP_DIM, POOL_GROUP_DIM), POOL_GROUP_DIM ** -0.5),
        'pool_scale': 1.0 + 0.1 * jax.random.normal(ks[14], (L_, POOL_WIDTH), F32),
        'mix_norm_g': gain(ks[15], (L_, D_MODEL)),
        'w_out': n(ks[16], (L_, D_MODEL, D_MODEL), D_MODEL ** -0.5),
        'norm2_g': gain(ks[17], (L_, D_MODEL)),
        'w_router': n(ks[18], (L_, D_MODEL, N_EXPERTS), D_MODEL ** -0.5),
        'w_gate': n(ks[19], (L_, N_EXPERTS, D_MODEL, EXPERT_FF), D_MODEL ** -0.5),
        'w_up': n(ks[20], (L_, N_EXPERTS, D_MODEL, EXPERT_FF), D_MODEL ** -0.5),
        'w_down': n(ks[21], (L_, N_EXPERTS, EXPERT_FF, D_MODEL), EXPERT_FF ** -0.5),
        'final_g': gain(ks[22], (D_MODEL,)),
    }

def second_block(x, norm1_g, w_in, hy_short_w, hy_short_b, hy_f_w1, hy_f_b1, hy_f_w2, hy_f_b2,
              hy_f_wout, hy_f_freq, hy_skip, na_rpb, pool_w, pool_scale, mix_norm_g, w_out,
              norm2_g, w_router, w_gate, w_up, w_down, final_g):
    L = x.shape[1]
    cuts = [3 * HY_WIDTH, 3 * HY_WIDTH + NA_WIDTH, 3 * HY_WIDTH + 2 * NA_WIDTH,
            3 * HY_WIDTH + 3 * NA_WIDTH]
    for i in range(DEPTH_2):
        h = rms_norm_2(x, norm1_g[i])
        proj = h @ w_in[i]
        hy_in, q, k, v, pool_in = jnp.split(proj, cuts, axis=-1)
        filt = hyena_filter(L, hy_f_w1[i], hy_f_b1[i], hy_f_w2[i], hy_f_b2[i],
                            hy_f_wout[i], hy_f_freq[i])
        y_hy = hyena_mixer(hy_in, hy_short_w[i], hy_short_b[i], filt, hy_skip[i])
        y_na = neighbourhood_attention(q, k, v, na_rpb[i])
        y_pool = pool_mixer(pool_in, pool_w[i], pool_scale[i])
        g = mix_norm_g[i]
        mixed = jnp.concatenate([
            rms_norm_2(y_hy, g[:HY_WIDTH]),
            rms_norm_2(y_na, g[HY_WIDTH:HY_WIDTH + NA_WIDTH]),
            rms_norm_2(y_pool, g[HY_WIDTH + NA_WIDTH:])], axis=-1)
        x = x + mixed @ w_out[i]
        x = x + expert_choice_moe(rms_norm_2(x, norm2_g[i]), w_router[i], w_gate[i],
                                  w_up[i], w_down[i])
    return rms_norm_2(x, final_g)


def setup_inputs(seed=0):
    out = dict(first_inputs(seed))
    for name, value in second_inputs(seed + 1).items():
        if name != "x":
            out[name + "_2"] = value
    return out


def reference(
    x, p, norm_pre, norm_post, att_w_in, att_b_f, att_w_out, rec_w_in, rec_lb, rec_out_norm,
    rec_w_out, ple_w_proj, ple_w_gate, norm1_g_2, w_in_2, hy_short_w_2, hy_short_b_2, hy_f_w1_2,
    hy_f_b1_2, hy_f_w2_2, hy_f_b2_2, hy_f_wout_2, hy_f_freq_2, hy_skip_2, na_rpb_2, pool_w_2,
    pool_scale_2, mix_norm_g_2, w_out_2, norm2_g_2, w_router_2, w_gate_2, w_up_2, w_down_2,
    final_g_2,
):
    x = first_block(
        x, p, norm_pre, norm_post, att_w_in, att_b_f, att_w_out, rec_w_in, rec_lb, rec_out_norm,
        rec_w_out, ple_w_proj, ple_w_gate,
    )
    return second_block(
        x, norm1_g_2, w_in_2, hy_short_w_2, hy_short_b_2, hy_f_w1_2, hy_f_b1_2, hy_f_w2_2,
        hy_f_b2_2, hy_f_wout_2, hy_f_freq_2, hy_skip_2, na_rpb_2, pool_w_2, pool_scale_2,
        mix_norm_g_2, w_out_2, norm2_g_2, w_router_2, w_gate_2, w_up_2, w_down_2, final_g_2,
    )


_drawn_inputs = setup_inputs


def setup_inputs(seed=0):
    import zlib

    import numpy as np

    out = dict(_drawn_inputs(seed))
    spreads = {}
    factors = {'norm1_g_2': 3.758,
     'hy_short_b_2': 5.734,
     'hy_f_b1_2': 7.269,
     'hy_f_b2_2': 6.978,
     'hy_f_freq_2': 8.0,
     'na_rpb_2': 8.0,
     'mix_norm_g_2': 5.281,
     'norm2_g_2': 6.831,
     'final_g_2': 2.952}
    for name, (base, spread) in spreads.items():
        noise = np.random.default_rng([zlib.crc32(name.encode()), seed]).standard_normal(out[name].shape)
        drawn = base * np.exp(spread * noise) if base else spread * noise
        out[name] = __import__('jax').numpy.asarray(drawn.astype(out[name].dtype))
    for name, factor in factors.items():
        out[name] = (out[name] * factor).astype(out[name].dtype)
    return out
```

```python
from contextlib import ExitStack

import numpy as np

import concourse.bass as bass
from concourse import mybir

F32 = mybir.dt.float32
I32 = mybir.dt.int32
ALU = mybir.AluOpType
ACT = mybir.ActivationFunctionType
AX = mybir.AxisListType.X

P = 128
T = 512
TT = T // P
D = 1024
KT = D // P
EPS = 1e-6
AH, AD = 16, 64
RH = 8
LEVELS = 7
NH = 8
GW = 64
RPB_ROWS, RPB_COLS = 15, 31
NE = 16
CAP = 64
FF = 2048
PAIRS = NE // 2
NEG = -1.0e30
MAGIC = 12582912.0
TWO_PI_HI = 6.28125
TWO_PI_LO = 0.0019353071795864769
PI_IN = 3.1415925


def constants():
    ident = np.eye(P, dtype=np.float32)
    causal = np.zeros((P, T), np.float32)
    r = np.arange(P)
    causal[:, T - P:] = np.where(r[None, :] > r[:, None], NEG, 0.0)
    reset = np.ones((P, T), np.float32)
    reset[:, ::P] = 0.0
    cols = np.arange(GW)
    start = np.clip(cols - 8, 0, GW - 16)
    inside = (cols[None, :] >= start[:, None]) & (cols[None, :] < start[:, None] + 16)
    window = np.where(inside, 0.0, NEG).astype(np.float32)
    window = np.concatenate([window, window], axis=0)
    slots = np.broadcast_to(np.arange(1, CAP + 1, dtype=np.float32), (P, CAP))
    table = np.concatenate([ident, causal, reset, window, slots], axis=1)

    masks = np.zeros((P, LEVELS, P // 2), np.int32)
    for level in range(LEVELS):
        half = 1 << level
        s = np.arange(P)
        left = (s // half) % 2 == 0
        block = s // (2 * half)
        t = np.arange(P // 2)
        masks[:, level, :] = left[:, None] & (block[:, None] == (t // half)[None, :])

    n = np.arange(T, dtype=np.float64)
    angle = 2.0 * np.pi * np.outer(n, n + 0.5) / (2 * T)
    dft = np.stack([np.cos(angle), np.sin(angle), np.cos(angle).T, np.sin(angle).T])

    lin = np.linspace(0.0, 1.0, T)
    bands = np.linspace(1e-4, 15.0, 16)
    ang = 2.0 * np.pi * n / T
    z = np.concatenate([lin[None, :], np.cos(bands[:, None] * ang), -np.sin(bands[:, None] * ang)])
    deltas = np.abs(np.linspace(np.log(1e-2) / 0.3, np.log(1e-2) / 1.5, 256))
    decay = np.exp(-lin[:, None] * deltas[None, :])
    decay = np.concatenate([decay, decay], axis=1)
    decay[0, 256:] = 0.0

    inv = np.zeros((256, T), np.float32)
    for g, w in enumerate((2, 4, 8, 16)):
        lo, hi = np.clip(n - w // 2, 0, T), np.clip(n + w // 2, 0, T)
        inv[64 * g:64 * g + 64] = (1.0 / (hi - lo)).astype(np.float32)
    f = lambda a: np.ascontiguousarray(a, dtype=np.float32)
    return {"table": f(table), "masks": masks.reshape(P, -1), "dft": f(dft), "filter_z": f(z),
            "decay": f(decay), "inv_count": f(inv)}


class Ledger:

    def __init__(self, jobs, banks, by_act, by_dve):
        self.jobs, self.banks = jobs, banks
        self.drain_sem = {"act": by_act, "dve": by_dve}
        self.index = {name: j for j, (name, _) in enumerate(jobs)}
        assert len(self.index) == len(jobs)
        self.total = {"act": 0, "dve": 0}
        self.rank, self.reader = {}, {}
        for name, who in jobs:
            self.total[who] += 1
            self.rank[name], self.reader[name] = self.total[who], who

    def bank(self, name):
        return self.banks[self.index[name] % 8]

    def nth(self, name):
        return self.index[name] + 1

    def drained(self, name):
        return self.drain_sem[self.reader[name]], self.rank[name]

    def reused(self, name):
        return self.index[name] >= 8

    def freed(self, name):
        return self.drained(self.jobs[self.index[name] - 8][0])


def turn(n):
    return "act" if n % 2 == 0 else "dve"


def psum_jobs():
    def norm(tag):
        for k in range(KT):
            yield (tag, k), turn(k)

    def halves(tag, who):
        for half in range(2):
            for i in range(TT):
                yield (tag, half, i), (turn(i) if who is None else who)

    def tail(layer):
        yield from norm(("mixed", layer))
        yield from halves(("out", layer), "dve")
        yield from norm(("h", layer))
        yield from halves(("gate", layer), "act")
        yield from halves(("ple", layer), "dve")

    yield from norm("u0")
    yield ("forget",), "dve"
    for m in range(8):
        yield ("q0", m), "act"
    for m in range(8):
        yield ("k0", m), "dve"
    yield from halves("v0", None)
    yield from halves("g0", "act")
    for h in range(AH + 1):
        if h < AH:
            for i in range(TT):
                yield ("s0", h, i), "dve"
        if h >= 1:
            for i in range(TT):
                yield ("pt0", h - 1, i), "act"
            yield ("o0", h - 1), "dve"
    yield from tail(0)

    yield from norm("u1")
    for h in range(RH):
        yield ("f1", h), "dve"
    for m in range(8):
        yield ("q1", m), "act"
    yield from halves("i1", "act")
    yield from halves("g1", "act")
    for h in range(RH):
        yield ("diag", h), "dve"
        for level in range(LEVELS):
            yield ("level", h, level), "dve"
        yield ("kw", h), "act"
        for c in range(TT - 1):
            yield ("state", h, c), "dve"
        yield ("o1", h), "dve"
    yield from tail(1)

    yield from norm("u2")
    yield ("fh1",), "dve"
    for m in range(6):
        yield ("hy", m), "act"
    yield ("fh2",), "dve"
    for m in range(4):
        yield ("q2", m), "act"
    for m in range(4):
        yield ("k2", m), "dve"
    for i in range(TT):
        yield ("v2", i), "act"
    for m in range(2):
        yield ("pool", m), "act"
    for i in range(TT):
        yield ("fh3", i), "dve"
    for k in range(TT):
        yield ("H", k), "act"
    for i in range(TT):
        yield ("zt", i), "act"
    for k in range(TT):
        yield ("Z", k), "act"
    for i in range(TT):
        yield ("pooled", i), "dve"
    for m in range(2):
        yield ("conv", m), "dve"
    for i in range(TT):
        yield ("yh", i), "act"
    for h in range(NH + 1):
        if h < NH:
            for i in range(TT):
                yield ("s2", h, i), "dve"
        if h >= 1:
            for i in range(TT):
                yield ("pt2", h - 1, i), "act"
            yield ("o2", h - 1), "dve"
    yield from norm("mix")
    yield from halves("out2", "dve")
    yield from norm("u3")
    yield ("router",), "dve"
    yield ("aff",), "dve"
    yield ("slot",), "dve"


def moe_jobs():
    for half in range(2):
        yield ("xs", half), "dve"
    for e in range(2):
        for f in range(4):
            yield ("gate", e, f), "act"
            yield ("up", e, f), "dve"
        for half in range(2):
            yield ("down", e, half), "act"
    for half in range(2):
        yield ("yrow", half), "act"
    yield ("spread",), "act"
    for half in range(2):
        for i in range(TT):
            yield ("add", half, i), "dve"


def two_blocks(nc, a, out):
    ctx = ExitStack()
    with ctx:
        def sb(name, cols, dt=F32, rows=P):
            return ctx.enter_context(nc.sbuf_tensor(name, [rows, cols], dt))

        def sem(name):
            return ctx.enter_context(nc.semaphore(name))

        arena = sb("arena", 49152)

        def cut(off, *dims, rows=P):
            n = int(np.prod(dims))
            v = arena[0:rows, off:off + n]
            if len(dims) == 2:
                return v.rearrange("p (a b) -> p a b", a=dims[0])
            if len(dims) == 3:
                return v.rearrange("p (a b c) -> p a b c", a=dims[0], b=dims[1])
            return v

        SLAB = 4096
        RING = 2
        H = cut(0, TT, D)
        ring = [SLAB * (1 + s) for s in range(6)]
        moe_ring = ring[2:] + ring[:2]
        UT = cut(12288, KT, T)
        q0 = cut(16384, AH, T, rows=AD + 1)
        k0 = cut(24576, AH, T, rows=AD + 1)
        v0 = cut(32768, TT, D)
        g0 = cut(36864, TT, D)
        U0 = cut(36864, TT, D)
        tri = [0, 128, 384, 768]
        prob0 = [12288, 12288 + 1280]
        pt0 = 12288 + 2560
        mixT0, y0, hT0, gate0 = cut(16384, KT, T), cut(20480, TT, D), cut(24576, KT, T), cut(28672, TT, D)
        logf0 = [cut(40960 + T * n, T, rows=AH) for n in range(4)]
        q1, k1, b1 = cut(16384, RH, T), cut(20480, RH, T), cut(24576, RH, T)
        i1, g1, U1 = cut(28672, TT, D), cut(32768, TT, D), cut(32768, TT, D)
        expo = [cut(12288, LEVELS, T), cut(36864, LEVELS, T)]
        kl1 = cut(40448, LEVELS, T)
        sT1 = [cut(44032, TT, P), cut(44544, TT, P)]
        qd1, kd1 = cut(45056, T), cut(45568, T)
        kw1, st1, oraw1, osq1 = cut(46080, 3, P), cut(46464, 3, P), cut(46848, TT, P), cut(47360, TT, P)
        fwork = [[cut(36864 + 4096 * s + T * n, T) for n in range(7)] for s in range(2)]
        mixT1, y1, hT1, gate1 = mixT0, y0, hT0, gate0
        U2 = cut(38912, TT, D)
        dft = [cut(16384 + 2048 * n, TT, T) for n in range(4)]
        hy = cut(24576, 6, T + 2)
        q2, k2 = cut(28672, NH, T, rows=AD), cut(32768, NH, T, rows=AD)
        v2 = cut(36864, TT, T)
        mix = cut(38912, TT, D)
        fh = cut(43008, TT, T)
        hs = cut(45056, TT, T)
        zrow = cut(47104, TT, 256)
        tmpA, tmpB = cut(48128, T), cut(48640, T)
        tmp2 = cut(48128, TT, 256)
        decay = cut(12288, TT, T)
        invc = cut(14336, 2, T)
        pdiff = cut(15360, 2, T)
        praw, psum_t = cut(38912, 2, T), cut(39936, 2, T + 16)
        prob2 = [12288, 14336]
        pt2 = cut(43008, TT, T)
        bias2 = [cut(45056, 14, GW), cut(46080, 14, GW)]
        raw2 = [cut(47104, 14, GW), cut(48128, 14, GW)]
        mixT2, mixsq2 = cut(28672, KT, T), cut(28672, TT, D)
        hn, hnT, onehot = cut(32768, TT, D), cut(36864, KT, T), cut(40960, TT, NE, CAP)
        affT, scratchT, selT, posT = [cut(45056 + T * n, T, rows=NE) for n in range(4)]
        w28, w36 = 28672, 36864
        ohp, gop = cut(w28, TT, P), cut(w28 + 512, TT, P)
        xs = cut(w28 + 1024, KT, P)
        act_t = [cut(w28 + 2048 + 256 * n, 256) for n in range(2)]
        hT = [cut(w36 + 1024 * n, 16, CAP) for n in range(2)]
        yT = cut(w36 + 2048, KT, P)
        yrow = cut(w28 + 2560, D)
        ohT = cut(w36 + 3072, T)

        tab = sb("tab", P + T + T + GW + CAP)
        ident, causal, reset = tab[:, 0:P], tab[:, P:P + T], tab[:, P + T:P + 2 * T]
        window, slots = tab[:, P + 2 * T:P + 2 * T + GW], tab[:, P + 2 * T + GW:P + 2 * T + GW + CAP]
        maskt = sb("maskt", LEVELS * 64, I32)
        cols = sb("cols", 90)
        gain_u = [cols[:, 0:8], cols[:, 8:16], cols[:, 16:24], cols[:, 24:32]]
        gain_mix = cols[:, 32:40]
        hyw = [cols[:, 40 + 6 * n:46 + 6 * n] for n in range(4)]
        skip = cols[:, 64:66]
        lb0, lb1 = cols[:, 66:74], cols[:, 74:82]
        small = sb("small", 272)
        ss, rstd = small[:, 0:12], small[:, 12:24]
        mx = small[:, 24:32]
        nmx = small[:, 32:40]
        rs = small[:, 40:48]
        rinv = small[:, 48:52]
        lw = [small[:, 52 + 8 * n:60 + 8 * n] for n in range(5)]
        eb1 = small[:, 92:96]
        aff = small[:, 96:160]
        pos = small[:, 160:224]
        rmax, rsumr = small[:, 224:228], small[:, 228:232]
        top8 = small[0:NE, 232:240]
        mean, root = small[:, 240:252], small[:, 252:264]
        wfl = sb("wfl", KT * AH)
        w_small = wfl[:, :].rearrange("p (k n) -> p k n", k=KT)
        bf = sb("bf", 1)
        fpar = sb("fpar", 3)
        row = sb("row", D)
        rgain = sb("rgain", P)
        pscale = sb("pscale", 256)
        poolw = sb("poolw", 2 * P)
        fw = sb("fw", 64 + 64)
        fwork2 = [cut(45056 + T * n, T, rows=64) for n in range(4)]
        zc, fwout = cut(47104, T, rows=33), cut(47616, T, rows=64)

        banks = [ctx.enter_context(nc.psum_tensor(f"bank{n}", [P, T], F32)) for n in range(8)]

        filled, by_act, by_dve = sem("filled"), sem("drained_act"), sem("drained_dve")
        led = Ledger(list(psum_jobs()), banks, by_act, by_dve)
        nth, drained = led.nth, led.drained
        dve_step, forget_logs = sem("dve_step"), sem("forget_logs")

        x_loaded, tab_loaded = sem("x_loaded"), sem("tab_loaded")
        misc = sem("misc_loaded")
        squares = sem("squares_summed")
        scaled = sem("rows_scaled")
        mean_ready, root_out = sem("mean_square_ready"), sem("root_ready")
        h_ready = sem("h_updated")

        slabs = []

        def slab(name, src, kt, n, last):
            slabs.append((name, src, kt, n, last))

        def w_cols(w, c0, n):
            return w[:, c0:c0 + n].rearrange("(k p) n -> p k n", p=P)

        wa, wr, wi = a["att_w_in"], a["rec_w_in"], a["w_in_2"]
        for s in range(2):
            slab(("q0", s), w_cols(wa, 512 * s, 512), KT, 512, ("q0", 4 * s + 3))
        for s in range(2):
            slab(("k0", s), w_cols(wa, D + 512 * s, 512), KT, 512, ("k0", 4 * s + 3))
        for s in range(2):
            slab(("v0", s), w_cols(wa, 2 * D + 512 * s, 512), KT, 512, ("v0", s, 3))
        for s in range(2):
            slab(("g0", s), w_cols(wa, 3 * D + 512 * s, 512), KT, 512, ("g0", s, 3))

        def tail_slabs(layer, w_out):
            for s in range(2):
                slab(("out", layer, s), w_cols(w_out, 512 * s, 512), KT, 512, (("out", layer), s, 3))
            for s in range(2):
                slab(("gate", layer, s), w_cols(a["ple_w_gate"][layer], 512 * s, 512), KT, 512,
                     (("gate", layer), s, 3))
            slab(("ple", layer), a["ple_w_proj"][layer].rearrange("(k p) n -> p k n", p=P), 2, D,
                 (("ple", layer), 1, 3))

        tail_slabs(0, a["att_w_out"])
        for s in range(2):
            slab(("f1", s), w_cols(wr, D + 512 * s, 512), KT, 512, ("f1", 4 * s + 3))
        for s in range(2):
            slab(("q1", s), w_cols(wr, 512 * s, 512), KT, 512, ("q1", 4 * s + 3))
        for s in range(2):
            slab(("i1", s), w_cols(wr, 2 * D + 512 * s, 512), KT, 512, ("i1", s, 3))
        for s in range(2):
            slab(("g1", s), w_cols(wr, 3 * D + 512 * s, 512), KT, 512, ("g1", s, 3))
        tail_slabs(1, a["rec_w_out"])
        slab(("hy", 0), w_cols(wi, 0, 512), KT, 512, ("hy", 3))
        slab(("hy", 1), w_cols(wi, 512, 256), KT, 256, ("hy", 5))
        slab(("q2", 0), w_cols(wi, 768, 512), KT, 512, ("q2", 3))
        slab(("k2", 0), w_cols(wi, 1280, 512), KT, 512, ("k2", 3))
        slab(("v2", 0), w_cols(wi, 1792, 512), KT, 512, ("v2", 3))
        slab(("pool", 0), w_cols(wi, 2304, 256), KT, 256, ("pool", 1))
        for s in range(2):
            slab(("out2", s), w_cols(a["w_out_2"], 512 * s, 512), KT, 512, ("out2", s, 3))
        slab_at = {s[0]: n for n, s in enumerate(slabs)}
        slab_loaded = [sem(f"slab_loaded{s}") for s in range(RING)]

        def slab_view(name):
            n = slab_at[name]
            _, _, kt, cols_, _ = slabs[n]
            return cut(ring[n % RING], kt, cols_)

        def need_slab(pe, name):
            n = slab_at[name]
            pe.wait_ge(slab_loaded[n % RING], 16 * (n // RING + 1))
            return slab_view(name)

        H_AT = {}
        total = 0
        for name, n in (("mix0", 4), ("ple0", 8), ("mix1", 4), ("ple1", 8)):
            total += n
            H_AT[name] = total

        moe_names = list(moe_jobs())
        MJ = {name: k for k, (name, _) in enumerate(moe_names)}
        MREAD = dict(moe_names)
        MN = len(moe_names)
        mrank, mcount = {}, {"act": 0, "dve": 0}
        for name, who in moe_names:
            mcount[who] += 1
            mrank[name] = mcount[who]
        FILL0 = len(led.jobs)

        def pair_nth(p, name):
            return p * MN + (FILL0 + MJ[name] + 1)

        def pair_drained(p, name, back=0):
            who = MREAD[name]
            return led.drain_sem[who], p * mcount[who] + (led.total[who] + mrank[name] - back * mcount[who])

        def pair_bank(name):
            return banks[MJ[name] % 8]

        pair_oh, half_read = sem("pair_onehot_ready"), sem("down_slab_read")
        mslab = [sem(f"expert_slab{s}") for s in range(6)]
        h_bias = [sem(f"bias_loaded{n}") for n in range(2)]
        scratch_written = sem("scratch_written")
        dma_row = sem("row_loaded")
        out_written = sem("out_written")
        loop_ready = sem("onehot_ready")
        pT_loaded = sem("p_loaded")
        dft_loaded, decay_loaded = sem("dft_loaded"), sem("decay_loaded")
        router_loaded = sem("router_loaded")
        zc_loaded = sem("zc_loaded")
        negc_loaded = sem("forget_row_loaded")
        negc_ready = sem("forget_ready")
        ones_set = sem("ones_set")
        scores_in, probs_in = sem("scores_shifted"), sem("probs_ready")
        logs = sem("forget_steps")
        f_dve, f_act = sem("f1_dve"), sem("f1_act")
        g_scaled = sem("g1_scaled")
        expo_in, expo_done, decayed = sem("exponents_ready"), sem("exponentials_ready"), sem("decayed_ready")
        last_in, last_done, gated = sem("chunk_exponents_ready"), sem("chunk_exponentials_ready"), sem("o1_gated")
        kl_zero = sem("left_zeroed")
        o_sq = sem("o1_squares")
        lb_dve, lb_act = sem("lb_dve"), sem("lb_act")
        sin_in, sin_out = sem("sine_in"), sem("sine_out")
        z_ready, prod_ready = sem("z_ready"), sem("product_ready")
        pool_ready, fsum = sem("pool_ready"), sem("filter_sums")
        yh_ready = sem("yh_ready")
        hy_edges, poolw_zero = sem("hy_edges"), sem("pool_weights_zeroed")
        mixed_ready = sem("mixed_ready")
        y_scaled = sem("y_scaled")
        rt_in, rt_exp, rt_out = sem("router_shifted"), sem("router_exponentials"), sem("affinities_ready")
        poolw_loaded = sem("pool_weights_loaded")
        final_in = sem("final_rows")

        pT = cut(32768, 2, T)

        block = ctx.enter_context(nc.Block())

        @block.sync
        def _(sp):
            for n, (name, src, kt, ncols, _) in enumerate(slabs):
                if n >= RING:
                    sp.wait_ge(filled, nth(slabs[n - RING][4]))
                sp.dma_start(cut(ring[n % RING], kt, ncols), src).then_inc(slab_loaded[n % RING], 16)
            def expert_loads(p):
                for e in range(2):
                    ei = p * 2 + e
                    wg, wu, wd = (a[w][bass.ds(ei, 1), :, :].rearrange("e (k p) n -> p (e k) n", p=P)
                                  for w in ("w_gate_2", "w_up_2", "w_down_2"))
                    order = [w for f in range(4) for w in ((wg, f), (wu, f))]
                    for n, (w, f) in enumerate(order):
                        yield 12 * e + n, w[:, :, 512 * f:512 * f + 512]
                    for half in range(2):
                        for kh in range(2):
                            yield 12 * e + 8 + 2 * half + kh, wd[:, 8 * kh:8 * kh + 8, 512 * half:512 * half + 512]

            def slab_free(k, p):
                e, n = divmod(k, 12)
                if n < 8:
                    sp.wait_ge(filled, pair_nth(p, (("gate", "up")[n % 2], e, n // 2)))
                elif n % 2 == 0:
                    sp.wait_ge(half_read, p * 4 + (2 * e + (n - 8) // 2 + 1))
                else:
                    sp.wait_ge(filled, pair_nth(p, ("down", e, (n - 8) // 2)))

            sp.wait_ge(filled, nth(("o2", NH - 1)))
            for k, src in expert_loads(0):
                if k == 4:
                    sp.wait_ge(filled, nth(("out2", 1, 3)))
                if k >= 6:
                    slab_free(k - 6, 0)
                sp.dma_start(cut(moe_ring[k % 6], 8, 512), src).then_inc(mslab[k % 6], 16)
            with sp.Fori(1, PAIRS) as p:
                for k, src in expert_loads(p):
                    if k >= 6:
                        slab_free(k - 6, p)
                    else:
                        slab_free(k + 18, p - 1)
                    sp.dma_start(cut(moe_ring[k % 6], 8, 512), src).then_inc(mslab[k % 6], 16)
            sp.wait_ge(final_in, 4)
            sp.dma_start(out.rearrange("(i p) d -> p i d", p=P), cut(w28, TT, D)).then_inc(out_written, 16)
            sp.wait_ge(out_written, 16)

        @block.gpsimd
        def _(pool):
            pool.dma_start(H, a["x"].rearrange("(i p) d -> p i d", p=P)).then_inc(x_loaded, 16)
            pool.dma_start(tab[:, :], a["table"]).then_inc(tab_loaded, 16)
            pool.dma_start(cols[:, :], a["cols"]).then_inc(tab_loaded, 16)
            pool.dma_start(w_small, w_cols(wa, 4 * D, AH)).then_inc(tab_loaded, 16)
            pool.dma_start(bf[0:AH, :], a["att_b_f"]).then_inc(tab_loaded, 16)
            pool.dma_start(maskt[:, :], a["masks"]).then_inc(misc, 16)
            pool.dma_start(fpar[0:64, :], a["filter_params"]).then_inc(misc, 16)
            pool.dma_start(fw[0:33, 0:64], a["hy_f_w1_2"]).then_inc(misc, 16)
            pool.dma_start(fw[0:64, 64:128], a["hy_f_w2_2"]).then_inc(misc, 16)
            pool.dma_start(rgain[:, :], a["rec_out_norm"].partition_broadcast(P)).then_inc(misc, 16)
            pool.dma_start(pscale[:, :], a["pool_scale_2"].partition_broadcast(P)).then_inc(misc, 16)
            R = NH * RPB_ROWS * RPB_COLS
            flat = a["na_rpb_2"]
            for dst0, src0, n in ((64, 0, R), (0, 0, 64), (64 + R, 0, 64)):
                pool.dma_start(a["rpb_padded"][dst0:dst0 + n].rearrange("(o n) -> o n", o=1),
                               flat[src0:src0 + n].rearrange("(o n) -> o n", o=1)).then_inc(scratch_written, 16)
            pool.memset(q0[AD:AD + 1, :, :], 1.0).then_inc(ones_set, 1)
            pool.wait_ge(ones_set, 1)
            pool.memset(poolw[:, :], 0.0).then_inc(poolw_zero, 1)
            pool.wait_ge(poolw_zero, 1)
            for g in range(4):
                r0 = 64 * (g % 2)
                pool.dma_start(poolw[r0:r0 + 64, P * (g // 2) + r0:P * (g // 2) + r0 + 64],
                               a["pool_w_2"][g]).then_inc(poolw_loaded, 16)
            pool.wait_ge(negc_ready, 1)
            for h in range(AH):
                pool.dma_start(k0[AD:AD + 1, h, :], logf0[3][h:h + 1, :]).then_inc(negc_loaded, 16)

            def load_row(src):
                pool.dma_start(row[:, :], src.partition_broadcast(P)).then_inc(dma_row, 16)

            def load_p(layer):
                pool.dma_start(pT, a["p"][layer].rearrange("(k p) t -> p k t", p=P)).then_inc(pT_loaded, 16)

            load_row(a["norm_post"][0])
            pool.wait_ge(filled, nth(("o0", AH - 1)))
            load_p(0)

            pool.wait_ge(filled, nth(("g1", 1, 3)))
            pool.wait_ge(f_dve, 4 * RH)
            pool.memset(kl1, 0.0).then_inc(kl_zero, 1)
            pool.wait_ge(kl_zero, 1)
            pool.wait_ge(y_scaled, 4)
            load_row(a["norm_post"][1])
            pool.wait_ge(*drained(("q1", 7)))
            pool.wait_ge(f_act, 6 * RH)
            for h in range(RH):
                e = expo[h % 2]
                pool.wait_ge(expo_done, h + 1)
                if h >= 1:
                    pool.wait_ge(filled, nth(("level", h - 1, LEVELS - 1)))
                for level in range(LEVELS):
                    half = 1 << level
                    ev = e[:, level, :].rearrange("p (n g s) -> p n g s", g=2, s=half)
                    qv = q1[:, h, :].rearrange("p (n g s) -> p n g s", g=2, s=half)
                    kv = k1[:, h, :].rearrange("p (n g s) -> p n g s", g=2, s=half)
                    lv = kl1[:, level, :].rearrange("p (n g s) -> p n g s", g=2, s=half)
                    pool.tensor_tensor(ev[:, :, 1, :], ev[:, :, 1, :], qv[:, :, 1, :], ALU.mult
                                       ).then_inc(decayed, 1)
                    pool.tensor_tensor(lv[:, :, 0, :], ev[:, :, 0, :], kv[:, :, 0, :], ALU.mult
                                       ).then_inc(decayed, 1)
                pool.wait_ge(last_done, 3 * h + 3)
                pool.tensor_tensor(qd1, qd1, q1[:, h, :], ALU.mult).then_inc(decayed, 1)
                pool.tensor_tensor(kd1[:, 0:384], kd1[:, 0:384], k1[:, h, 0:384], ALU.mult).then_inc(decayed, 1)
            pool.wait_ge(filled, nth((("mixed", 1), 7)))
            load_p(1)

            pool.wait_ge(h_ready, H_AT["ple1"])
            pool.wait_ge(filled, nth((("ple", 1), 1, 3)))
            pool.memset(hy[:, :, 0:1], 0.0).then_inc(hy_edges, 1)
            pool.memset(hy[:, :, T + 1:T + 2], 0.0).then_inc(hy_edges, 1)
            for n in range(4):
                pool.dma_start(dft[n], a["dft"][n].rearrange("(k p) n -> p k n", p=P)).then_inc(dft_loaded, 16)
            pool.dma_start(w_small, a["w_router_2"].rearrange("(k p) n -> p k n", p=P)).then_inc(router_loaded, 16)
            pool.wait_ge(filled, nth(("u2", 7)))
            pool.dma_start(zc, a["filter_z"]).then_inc(zc_loaded, 16)
            pool.dma_start(fwout, a["hy_f_wout_2"]).then_inc(zc_loaded, 16)
            pool.wait_ge(filled, nth(("pool", 1)))
            pool.dma_start(decay, a["decay"].rearrange("(k p) n -> p k n", p=P)).then_inc(decay_loaded, 16)
            pool.dma_start(invc, a["inv_count"].rearrange("(k p) n -> p k n", p=P)).then_inc(decay_loaded, 16)
            pool.wait_ge(y_scaled, 8)
            load_row(a["final_g_2"])
            pool.wait_ge(filled, nth(("conv", 1)))
            pool.wait_ge(scratch_written, 48)
            for h in range(NH):
                if h >= 2:
                    pool.wait_ge(*drained(("s2", h - 2, 0)))
                for par in range(2):
                    src = bass.AP(a["rpb_padded"].tensor,
                                  64 + RPB_COLS * (h * RPB_ROWS + 1 - par) - 48,
                                  [[1, GW], [RPB_COLS, 14], [1, GW]])
                    pool.dma_start(raw2[h % 2][64 * par:64 * par + 64, :, :], src).then_inc(h_bias[h % 2], 16)

        @block.tensor
        def _(pe):
            def transposes(tag, src, wait):
                for k in range(KT):
                    if led.reused((tag, k)):
                        pe.wait_ge(*led.freed((tag, k)))
                    bank = led.bank((tag, k))
                    for i in range(TT):
                        if k == 0:
                            wait(i)
                        mm = pe.transpose(bank[:, P * i:P * i + P], src[:, i, P * k:P * k + P], ident)
                    mm.then_inc(filled, 1)

            def channel_major(tag, m, w, c, xT):
                pe.wait_ge(*led.freed((tag, m)))
                bank = led.bank((tag, m))
                for k in range(KT):
                    mm = pe.matmul(bank[:, :], w[:, k, c:c + P], xT[:, k, :], start=(k == 0), stop=(k == KT - 1))
                mm.then_inc(filled, 1)

            def token_major(name, w, xT, i, c=0, n=512, kt=KT):
                pe.wait_ge(*led.freed(name))
                bank = led.bank(name)
                for k in range(kt):
                    mm = pe.matmul(bank[:, 0:n], xT[:, k, P * i:P * i + P], w[:, k, c:c + n],
                                   start=(k == 0), stop=(k == kt - 1))
                mm.then_inc(filled, 1)

            def projection_cm(tag, slabs_, groups, xT):
                for m in range(groups):
                    if m % 4 == 0:
                        w = need_slab(pe, (tag, m // 4))
                    channel_major(tag, m, w, P * (m % 4), xT)

            def projection_tm(tag, slab_name, xT):
                for half in range(2):
                    w = need_slab(pe, (*slab_name, half))
                    for i in range(TT):
                        token_major((tag, half, i), w, xT, i)

            def after_all(tag):
                pe.wait_ge(*drained((tag, 6)))
                pe.wait_ge(*drained((tag, 7)))

            def tail(layer, mixed, mixedT, hT, ready):
                transposes(("mixed", layer), mixed, ready)
                after_all(("mixed", layer))
                projection_tm(("out", layer), ("out", layer), mixedT)
                transposes(("h", layer), H, lambda i: pe.wait_ge(h_ready, H_AT[f"mix{layer}"] - 3 + i))
                after_all(("h", layer))
                projection_tm(("gate", layer), ("gate", layer), hT)
                pe.wait_ge(pT_loaded, 16 * (layer + 1))
                w = need_slab(pe, ("ple", layer))
                for half in range(2):
                    for i in range(TT):
                        token_major((("ple", layer), half, i), w, pT, i, c=512 * half, kt=2)

            pe.wait_ge(tab_loaded, 64)
            transposes("u0", U0, lambda i: pe.wait_ge(scaled, i + 1))
            after_all("u0")
            pe.wait_ge(*led.freed(("forget",)))
            bank = led.bank(("forget",))
            for k in range(KT):
                mm = pe.matmul(bank[0:AH, :], w_small[:, k, :], UT[:, k, :], start=(k == 0), stop=(k == KT - 1))
            mm.then_inc(filled, 1)
            projection_cm("q0", 2, 8, UT)
            projection_cm("k0", 2, 8, UT)
            projection_tm("v0", ("v0",), UT)
            projection_tm("g0", ("g0",), UT)
            pe.wait_ge(ones_set, 1)
            pe.wait_ge(negc_loaded, 16 * AH)
            pe.wait_ge(*drained(("q0", 7)))
            pe.wait_ge(*drained(("k0", 7)))
            for h in range(AH + 1):
                if h < AH:
                    for i in range(TT):
                        n = P * (i + 1)
                        pe.wait_ge(*led.freed(("s0", h, i)))
                        bank = led.bank(("s0", h, i))
                        pe.matmul(bank[:, 0:n], q0[:, h, P * i:P * i + P], k0[:, h, 0:n],
                                           start=True, stop=True).then_inc(filled, 1)
                if h >= 1:
                    g = h - 1
                    for i in range(TT):
                        pe.wait_ge(probs_in, 4 * g + i + 1)
                        pe.wait_ge(*led.freed(("pt0", g, i)))
                        bank = led.bank(("pt0", g, i))
                        pr = cut(prob0[g % 2] + tri[i], P * (i + 1))
                        for j in range(i + 1):
                            mm = pe.transpose(bank[:, P * j:P * j + P], pr[:, P * j:P * j + P], ident)
                        mm.then_inc(filled, 1)
                    pe.wait_ge(*led.freed(("o0", g)))
                    bank = led.bank(("o0", g))
                    for i in range(TT):
                        pe.wait_ge(*drained(("pt0", g, i)))
                        pt = cut(pt0 + tri[i], P * (i + 1))
                        for j in range(i + 1):
                            mm = pe.matmul(bank[:, AD * i:AD * i + AD], pt[:, P * j:P * j + P],
                                           v0[:, j, AD * g:AD * g + AD], start=(j == 0), stop=(j == i))
                    mm.then_inc(filled, 1)
            tail(0, g0, mixT0, hT0, lambda i: pe.wait_ge(*drained(("o0", AH - 1))))

            transposes("u1", U1, lambda i: pe.wait_ge(scaled, 4 + i + 1))
            after_all("u1")
            projection_cm("f1", 2, 8, UT)
            projection_cm("q1", 2, 8, UT)
            projection_tm("i1", ("i1",), UT)
            projection_tm("g1", ("g1",), UT)
            pe.wait_ge(*drained(("q1", 7)))
            pe.wait_ge(f_act, 6 * RH)
            pe.wait_ge(*drained(("i1", 1, 3)))
            for h in range(RH):
                pe.wait_ge(*led.freed(("diag", h)))
                bank = led.bank(("diag", h))
                for c in range(TT):
                    mm = pe.matmul(bank[:, P * c:P * c + P], k1[:, h, P * c:P * c + P], q1[:, h, P * c:P * c + P],
                                   start=True, stop=True)
                mm.then_inc(filled, 1)
                for level in range(LEVELS):
                    half = 1 << level
                    pe.wait_ge(decayed, 16 * h + 2 * level + 2)
                    pe.wait_ge(*led.freed(("level", h, level)))
                    bank = led.bank(("level", h, level))
                    ev = expo[h % 2][:, level, :].rearrange("p (n g s) -> p n g s", g=2, s=half)
                    n = 64 // half
                    for c in range(TT):
                        mm = pe.matmul(bank[:, 64 * c:64 * c + 64], kl1[:, level, P * c:P * c + P],
                                       ev[:, n * c:n * c + n, 1, :], start=True, stop=True)
                    mm.then_inc(filled, 1)
                pe.wait_ge(decayed, 16 * h + 16)
                pe.wait_ge(*led.freed(("kw", h)))
                bank = led.bank(("kw", h))
                for c in range(TT - 1):
                    mm = pe.transpose(bank[:, P * c:P * c + P], kd1[:, P * c:P * c + P], ident)
                mm.then_inc(filled, 1)
                pe.wait_ge(*drained(("kw", h)))
                for c in range(TT - 1):
                    pe.wait_ge(*led.freed(("state", h, c)))
                    bank = led.bank(("state", h, c))
                    pe.matmul(bank[:, 0:P], kw1[:, c, :], i1[:, c, P * h:P * h + P], start=True, stop=True).then_inc(filled, 1)
                pe.wait_ge(*led.freed(("o1", h)))
                bank = led.bank(("o1", h))
                pe.wait_ge(*drained(("level", h, LEVELS - 1)))
                for c in range(TT):
                    mm = pe.matmul(bank[:, P * c:P * c + P], sT1[h % 2][:, c, :], i1[:, c, P * h:P * h + P],
                                   start=True, stop=(c == 0))
                    if c:
                        pe.wait_ge(*drained(("state", h, c - 1)))
                        mm = pe.matmul(bank[:, P * c:P * c + P], qd1[:, P * c:P * c + P], st1[:, c - 1, :],
                                       start=False, stop=True)
                mm.then_inc(filled, 1)
            tail(1, g1, mixT1, hT1, lambda i: pe.wait_ge(gated, 4 * RH))

            transposes("u2", U2, lambda i: pe.wait_ge(scaled, 8 + i + 1))
            after_all("u2")
            pe.wait_ge(misc, 96)
            pe.wait_ge(zc_loaded, 32)
            pe.wait_ge(*led.freed(("fh1",)))
            bank = led.bank(("fh1",))
            pe.matmul(bank[0:64, :], fw[0:33, 0:64], zc, start=True, stop=True).then_inc(filled, 1)
            projection_cm("hy", 2, 6, UT)
            pe.wait_ge(*led.freed(("fh2",)))
            bank = led.bank(("fh2",))
            pe.wait_ge(sin_out, 1)
            pe.matmul(bank[0:64, :], fw[0:64, 64:128], fwork2[3], start=True, stop=True).then_inc(filled, 1)
            projection_cm("q2", 1, 4, UT)
            projection_cm("k2", 1, 4, UT)
            w = need_slab(pe, ("v2", 0))
            for i in range(TT):
                token_major(("v2", i), w, UT, i)
            projection_cm("pool", 1, 2, UT)
            pe.wait_ge(sin_out, 2)
            for i in range(TT):
                pe.wait_ge(*led.freed(("fh3", i)))
                bank = led.bank(("fh3", i))
                pe.matmul(bank[:, :], fwork2[3][:, P * i:P * i + P], fwout,
                                   start=True, stop=True).then_inc(filled, 1)

            def analysis(tag, re_src, im_src, wait):
                pe.wait_ge(dft_loaded, 64)
                for k in range(TT):
                    if led.reused((tag, k)):
                        pe.wait_ge(*led.freed((tag, k)))
                    bank = led.bank((tag, k))
                    if k == 0:
                        wait()
                    for part, src in ((0, re_src), (1, im_src)):
                        for i in range(TT):
                            mm = pe.matmul(bank[:, 256 * part:256 * part + 256], dft[part][:, i, P * k:P * k + P],
                                           src(i), start=(i == 0), stop=(i == TT - 1))
                    mm.then_inc(filled, 1)

            analysis("H", lambda i: fh[:, i, 0:256], lambda i: fh[:, i, 256:512], lambda: pe.wait_ge(fsum, 4))
            pe.wait_ge(z_ready, 2)
            for i in range(TT):
                pe.wait_ge(*led.freed(("zt", i)))
                bank = led.bank(("zt", i))
                for m in range(2):
                    mm = pe.transpose(bank[:, P * m:P * m + P], hy[:, 2 + m, P * i:P * i + P], ident)
                mm.then_inc(filled, 1)
            analysis("Z", lambda i: zrow[:, i, :], lambda i: zrow[:, i, :], lambda: pe.wait_ge(*drained(("zt", 3))))
            pe.wait_ge(pool_ready, 4)
            pe.wait_ge(poolw_loaded, 64)
            for i in range(TT):
                pe.wait_ge(*led.freed(("pooled", i)))
                bank = led.bank(("pooled", i))
                for m in range(2):
                    mm = pe.matmul(bank[:, P * m:P * m + P], pdiff[:, m, P * i:P * i + P], poolw[:, P * m:P * m + P],
                                   start=True, stop=True)
                mm.then_inc(filled, 1)
            pe.wait_ge(prod_ready, 1)
            for m in range(2):
                pe.wait_ge(*led.freed(("conv", m)))
                bank = led.bank(("conv", m))
                for part, src in ((0, zrow), (1, tmp2)):
                    for k in range(TT):
                        mm = pe.matmul(bank[:, :], src[:, k, P * m:P * m + P], dft[2 + part][:, k, :],
                                       start=(part == 0 and k == 0), stop=(part == 1 and k == TT - 1))
                mm.then_inc(filled, 1)
            pe.wait_ge(yh_ready, 2)
            for i in range(TT):
                pe.wait_ge(*led.freed(("yh", i)))
                bank = led.bank(("yh", i))
                for m in range(2):
                    mm = pe.transpose(bank[:, P * m:P * m + P], hy[:, m, P * i:P * i + P], ident)
                mm.then_inc(filled, 1)
            pe.wait_ge(*drained(("q2", 3)))
            pe.wait_ge(*drained(("k2", 3)))
            for h in range(NH + 1):
                if h < NH:
                    for i in range(TT):
                        pe.wait_ge(*led.freed(("s2", h, i)))
                        bank = led.bank(("s2", h, i))
                        pe.matmul(bank[:, :], q2[:, h, P * i:P * i + P], k2[:, h, :], start=True, stop=True).then_inc(filled, 1)
                if h >= 1:
                    g = h - 1
                    for i in range(TT):
                        pe.wait_ge(probs_in, 4 * AH + 4 * g + i + 1)
                        pe.wait_ge(*led.freed(("pt2", g, i)))
                        bank = led.bank(("pt2", g, i))
                        pr = cut(prob2[g % 2] + T * i, T)
                        for j in range(TT):
                            mm = pe.transpose(bank[:, P * j:P * j + P], pr[:, P * j:P * j + P], ident)
                        mm.then_inc(filled, 1)
                    pe.wait_ge(*led.freed(("o2", g)))
                    bank = led.bank(("o2", g))
                    for i in range(TT):
                        pe.wait_ge(*drained(("pt2", g, i)))
                        for j in range(TT):
                            mm = pe.matmul(bank[:, AD * i:AD * i + AD], pt2[:, i, P * j:P * j + P],
                                           v2[:, j, AD * g:AD * g + AD], start=(j == 0), stop=(j == TT - 1))
                    mm.then_inc(filled, 1)
            transposes("mix", mix, lambda i: pe.wait_ge(mixed_ready, i + 1))
            after_all("mix")
            projection_tm("out2", ("out2",), mixT2)
            transposes("u3", hn, lambda i: pe.wait_ge(scaled, 12 + i + 1))
            after_all("u3")
            pe.wait_ge(router_loaded, 16)
            pe.wait_ge(*led.freed(("router",)))
            bank = led.bank(("router",))
            for i in range(TT):
                for k in range(KT):
                    mm = pe.matmul(bank[:, NE * i:NE * i + NE], hnT[:, k, P * i:P * i + P], w_small[:, k, :],
                                   start=(k == 0), stop=(k == KT - 1))
            mm.then_inc(filled, 1)
            pe.wait_ge(*led.freed(("aff",)))
            bank = led.bank(("aff",))
            pe.wait_ge(rt_out, 1)
            for i in range(TT):
                mm = pe.transpose(bank[0:NE, P * i:P * i + P], aff[:, NE * i:NE * i + NE], ident)
            mm.then_inc(filled, 1)
            pe.wait_ge(*led.freed(("slot",)))
            bank = led.bank(("slot",))
            pe.wait_ge(loop_ready, 1)
            for i in range(TT):
                mm = pe.transpose(bank[:, NE * i:NE * i + NE], posT[:, P * i:P * i + P], ident[0:NE, 0:NE])
            mm.then_inc(filled, 1)
            pe.wait_ge(by_act, led.total["act"])
            pe.wait_ge(by_dve, led.total["dve"])

            with pe.Fori(0, PAIRS) as p:
                def pair_freed(name):
                    k = MJ[name]
                    if k >= 8:
                        return pair_drained(p, moe_names[k - 8][0])
                    return pair_drained(p, moe_names[max(n for n in range(MN) if n % 8 == k)][0], back=1)

                def expert_slab(k):
                    pe.wait_ge(mslab[k % 6], p * 64 + 16 * (k // 6 + 1))
                    return cut(moe_ring[k % 6], 8, 512)

                pe.wait_ge(pair_oh, p * 2 + 1)
                for half in range(2):
                    pe.wait_ge(*pair_freed(("xs", half)))
                    bank = pair_bank(("xs", half))
                    for k in range(4):
                        kk = 4 * half + k
                        for i in range(TT):
                            mm = pe.matmul(bank[:, P * k:P * k + P], hn[:, i, P * kk:P * kk + P], ohp[:, i, :],
                                           start=(i == 0), stop=(i == TT - 1))
                    mm.then_inc(filled, 1)
                pe.wait_ge(*pair_drained(p, ("xs", 1)))
                for e in range(2):
                    for f in range(4):
                        for n, what in enumerate(("gate", "up")):
                            w = expert_slab(12 * e + 2 * f + n)
                            pe.wait_ge(*pair_freed((what, e, f)))
                            bank = pair_bank((what, e, f))
                            for m in range(4):
                                for k in range(KT):
                                    mm = pe.matmul(bank[:, CAP * m:CAP * m + CAP], w[:, k, P * m:P * m + P],
                                                   xs[:, k, CAP * e:CAP * e + CAP],
                                                   start=(k == 0), stop=(k == KT - 1))
                            mm.then_inc(filled, 1)
                    pe.wait_ge(*pair_drained(p, ("up", e, 3)))
                    for half in range(2):
                        pe.wait_ge(*pair_freed(("down", e, half)))
                        bank = pair_bank(("down", e, half))
                        for kh in range(2):
                            w = expert_slab(12 * e + 8 + 2 * half + kh)
                            for m in range(4):
                                for k in range(8):
                                    mm = pe.matmul(bank[:, CAP * m:CAP * m + CAP], w[:, k, P * m:P * m + P],
                                                   hT[e][:, 8 * kh + k, :],
                                                   start=(kh == 0 and m == 0 and k == 0),
                                                   stop=(kh == 1 and k == 7), skip_group_check=True)
                            if kh == 0:
                                mm.then_inc(half_read, 1)
                        mm.then_inc(filled, 1)
                pe.wait_ge(pair_oh, p * 2 + 2)
                pe.wait_ge(*pair_drained(p, ("down", 1, 1)))
                for half in range(2):
                    pe.wait_ge(*pair_freed(("yrow", half)))
                    bank = pair_bank(("yrow", half))
                    for k in range(4):
                        mm = pe.transpose(bank[:, P * k:P * k + P], yT[:, 4 * half + k, :], ident)
                    mm.then_inc(filled, 1)
                pe.wait_ge(*pair_freed(("spread",)))
                bank = pair_bank(("spread",))
                for i in range(TT):
                    mm = pe.transpose(bank[:, P * i:P * i + P], gop[:, i, :], ident)
                mm.then_inc(filled, 1)
                pe.wait_ge(*pair_drained(p, ("spread",)))
                for half in range(2):
                    for i in range(TT):
                        pe.wait_ge(*pair_freed(("add", half, i)))
                        bank = pair_bank(("add", half, i))
                        pe.matmul(bank[:, :], ohT[:, P * i:P * i + P], yrow[:, 512 * half:512 * half + 512],
                                  start=True, stop=True).then_inc(filled, 1)

        @block.scalar
        def _(act):
            def drain_groups(tag, dst, gain):
                for k in range(0, KT, 2):
                    act.wait_ge(filled, nth((tag, k)))
                    bank = led.bank((tag, k))
                    scale = 1.0 if gain is None else gain[:, k:k + 1]
                    act.activation(dst[:, k, :], bank[:, :], ACT.Identity, scale=scale).then_inc(by_act, 1)

            roots = [0]

            def square_root(c=4):
                roots[0] += 1
                act.wait_ge(mean_ready, roots[0])
                act.activation(root[:, 0:c], mean[:, 0:c], ACT.Sqrt).then_inc(root_out, 1)

            def squares_of(src, junk, ready):
                for i in range(TT):
                    ready(i)
                    act.activation(junk[:, i, :], src[:, i, :], ACT.Square, accum_out=ss[:, i:i + 1]
                                   ).then_inc(squares, 1)
                square_root()

            def copy(dst, name, src=None, scale=1.0, func=ACT.Identity):
                act.wait_ge(filled, nth(name))
                bank = led.bank(name)
                act.activation(dst, bank[:, :] if src is None else src(bank), func, scale=scale).then_inc(by_act, 1)

            def two_heads(dst, name, m, scale=1.0):
                act.wait_ge(filled, nth(name))
                bank = led.bank(name)
                act.activation(dst[0:AD, 2 * m, :], bank[0:AD, :], ACT.Identity, scale=scale)
                act.activation(dst[0:AD, 2 * m + 1, :], bank[AD:P, :], ACT.Identity, scale=scale).then_inc(by_act, 1)

            def softmax_exp(n, srcs):
                act.wait_ge(scores_in, n + 1)
                for i, s in enumerate(srcs):
                    r = 4 * (n % 2) + i
                    act.activation(s, s, ACT.Exp, bias=nmx[:, r:r + 1], accum_out=rs[:, r:r + 1]
                                   ).then_inc(probs_in, 1)

            def tail(layer, mixT, y, hT, gate):
                drain_groups(("mixed", layer), mixT, None)
                for i in range(TT):
                    act.wait_ge(*drained((("out", layer), 1, i)))
                    act.activation(gate[:, i, :], y[:, i, :], ACT.Square, accum_out=ss[:, i:i + 1]
                                   ).then_inc(squares, 1)
                square_root()
                drain_groups(("h", layer), hT, None)
                for half in range(2):
                    for i in range(TT):
                        copy(gate[:, i, 512 * half:512 * half + 512], (("gate", layer), half, i), func=ACT.Sigmoid)

            act.wait_ge(x_loaded, 16)
            act.wait_ge(tab_loaded, 64)
            squares_of(H, U0, lambda i: None)
            drain_groups("u0", UT, gain_u[0])
            act.wait_ge(logs, 1)
            act.activation(logf0[1], logf0[1], ACT.Exp).then_inc(forget_logs, 1)
            act.wait_ge(forget_logs, 1)
            act.activation(logf0[1], logf0[1], ACT.Ln, bias=1.0).then_inc(forget_logs, 1)
            for m in range(8):
                two_heads(q0, ("q0", m), m)
            for half in range(2):
                for i in range(0, TT, 2):
                    copy(v0[:, i, 512 * half:512 * half + 512], ("v0", half, i))
            act.wait_ge(filled, nth(("u0", 7)))
            for half in range(2):
                for i in range(TT):
                    copy(g0[:, i, 512 * half:512 * half + 512], ("g0", half, i), func=ACT.Silu)
            for h in range(AH + 1):
                if h < AH:
                    softmax_exp(h, [cut(prob0[h % 2] + tri[i], P * (i + 1)) for i in range(TT)])
                if h >= 1:
                    g = h - 1
                    if g >= 1:
                        act.wait_ge(filled, nth(("o0", g - 1)))
                    for i in range(TT):
                        copy(cut(pt0 + tri[i], P * (i + 1)), ("pt0", g, i), src=lambda b, i=i: b[:, 0:P * (i + 1)])
            tail(0, mixT0, y0, hT0, gate0)

            act.wait_ge(filled, nth((("ple", 0), 1, 3)))
            squares_of(H, U1, lambda i: act.wait_ge(h_ready, H_AT["ple0"] - 3 + i))
            drain_groups("u1", UT, gain_u[1])
            act.wait_ge(lb_dve, 2)
            act.activation(lw[2], lw[1], ACT.Exp).then_inc(lb_act, 1)
            act.wait_ge(lb_act, 1)
            act.activation(lw[2], lw[2], ACT.Ln, bias=1.0).then_inc(lb_act, 1)

            def gates_of(h):
                w = fwork[h % 2]
                act.wait_ge(f_dve, 4 * h + 1)
                act.activation(w[1], w[1], ACT.Exp).then_inc(f_act, 1)
                act.wait_ge(f_act, 6 * h + 1)
                act.activation(w[1], w[1], ACT.Ln, bias=1.0).then_inc(f_act, 1)
                act.wait_ge(f_dve, 4 * h + 3)
                act.activation(w[4], w[2], ACT.Abs, bias=lw[0][:, h:h + 1]).then_inc(f_act, 1)
                act.activation(k1[:, h, :], w[3], ACT.Exp, bias=lw[3][:, h:h + 1]).then_inc(f_act, 1)
                act.wait_ge(f_act, 6 * h + 3)
                act.activation(w[4], w[4], ACT.Exp, scale=-1.0).then_inc(f_act, 1)
                act.wait_ge(f_act, 6 * h + 5)
                act.activation(w[4], w[4], ACT.Ln, bias=1.0).then_inc(f_act, 1)

            for h in range(RH):
                gates_of(h)
            for m in range(8):
                copy(q1[:, m, :], ("q1", m))
            for half in range(2):
                for i in range(TT):
                    copy(i1[:, i, 512 * half:512 * half + 512], ("i1", half, i))
            for half in range(2):
                for i in range(TT):
                    copy(g1[:, i, 512 * half:512 * half + 512], ("g1", half, i), func=ACT.Silu)

            def level_exps(h):
                act.wait_ge(expo_in, h + 1)
                act.activation(expo[h % 2], expo[h % 2], ACT.Exp).then_inc(expo_done, 1)

            def chunk_exps(h):
                if h >= 1:
                    act.wait_ge(filled, nth(("o1", h - 1)))
                    act.wait_ge(*drained(("state", h - 1, 2)))
                act.activation(qd1, b1[:, h, :], ACT.Exp).then_inc(last_done, 1)
                act.activation(eb1, b1[:, h, :].rearrange("p (c t) -> p c t", c=TT)[:, :, P - 1], ACT.Exp
                               ).then_inc(last_done, 1)
                act.wait_ge(last_in, h + 1)
                act.activation(kd1[:, 0:384], kd1[:, 0:384], ACT.Exp).then_inc(last_done, 1)

            level_exps(0)
            chunk_exps(0)
            for h in range(RH):
                if h + 1 < RH:
                    level_exps(h + 1)
                copy(kw1[:, :, :], ("kw", h), src=lambda b: b[:, 0:384].rearrange("p (c t) -> p c t", c=3))
                if h + 1 < RH:
                    chunk_exps(h + 1)
                act.wait_ge(*drained(("o1", h)))
                if h >= 1:
                    act.wait_ge(gated, 4 * h)
                for i in range(TT):
                    act.activation(osq1[:, i, :], oraw1[:, i, :], ACT.Square, accum_out=ss[:, i:i + 1]
                                   ).then_inc(o_sq, 1)
                square_root()
            tail(1, mixT1, y1, hT1, gate1)

            squares_of(H, U2, lambda i: act.wait_ge(h_ready, H_AT["ple1"] - 3 + i))
            drain_groups("u2", UT, gain_u[2])

            def sine(n):
                act.wait_ge(sin_in, n)
                act.activation(fwork2[3], fwork2[0], ACT.Sin).then_inc(sin_out, 1)

            sine(1)
            act.wait_ge(hy_edges, 2)
            for m in range(6):
                copy(hy[:, m, 1:T + 1], ("hy", m))
            sine(2)
            for m in range(4):
                two_heads(q2, ("q2", m), m, scale=AD ** -0.5)
            for i in range(TT):
                copy(v2[:, i, :], ("v2", i))
            for m in range(2):
                copy(praw[:, m, :], ("pool", m))
            for k in range(TT):
                copy(hs[:, k, :], ("H", k), scale=1.0 / T)
            for i in range(TT):
                copy(zrow[:, i, :], ("zt", i), src=lambda b: b[:, 0:256])
            for k in range(TT):
                if k == 0:
                    act.wait_ge(filled, nth(("H", 3)))
                copy(fh[:, k, :], ("Z", k))
            act.wait_ge(pool_ready, 4)
            for i in range(TT):
                copy(mix[:, i, 0:256], ("yh", i), src=lambda b: b[:, 0:256])
            for h in range(NH + 1):
                if h < NH:
                    softmax_exp(AH + h, [cut(prob2[h % 2] + T * i, T) for i in range(TT)])
                if h >= 1:
                    g = h - 1
                    if g >= 1:
                        act.wait_ge(filled, nth(("o2", g - 1)))
                    for i in range(TT):
                        copy(pt2[:, i, :], ("pt2", g, i))
            act.wait_ge(*drained(("o2", NH - 1)))
            act.wait_ge(*drained(("pooled", 3)))
            act.wait_ge(*drained(("yh", 3)))
            for n, (c0, c1) in enumerate(((0, 256), (256, 768), (768, 1024))):
                for i in range(TT):
                    act.activation(mixsq2[:, i, c0:c1], mix[:, i, c0:c1], ACT.Square,
                                   accum_out=ss[:, 4 * n + i:4 * n + i + 1]).then_inc(squares, 1)
            square_root(12)
            drain_groups("mix", mixT2, gain_mix)
            squares_of(H, hn, lambda i: act.wait_ge(*drained(("out2", 1, i))))
            drain_groups("u3", hnT, gain_u[3])
            act.wait_ge(rt_in, 1)
            act.activation(aff, aff, ACT.Exp).then_inc(rt_exp, 1)

            act.wait_ge(loop_ready, 5)
            with act.Fori(0, PAIRS) as p:
                for e in range(2):
                    for f in range(4):
                        if f < 2:
                            if e == 1:
                                act.wait_ge(*pair_drained(p, ("up", 0, f + 2)))
                            else:
                                act.wait_ge(*pair_drained(p, ("up", 1, f + 2), back=1))
                        else:
                            act.wait_ge(*pair_drained(p, ("up", e, f - 2)))
                        act.wait_ge(filled, pair_nth(p, ("gate", e, f)))
                        bank = pair_bank(("gate", e, f))
                        act.activation(act_t[f % 2], bank[:, 0:256], ACT.Silu).then_inc(by_act, 1)
                    for half in range(2):
                        act.wait_ge(filled, pair_nth(p, ("down", e, half)))
                        bank = pair_bank(("down", e, half))
                        act.activation(yT[:, 4 * half:4 * half + 4, CAP * e:CAP * e + CAP],
                                               bank[:, 0:256].rearrange("p (m s) -> p m s", m=4), ACT.Identity).then_inc(by_act, 1)
                for half in range(2):
                    act.wait_ge(filled, pair_nth(p, ("yrow", half)))
                    bank = pair_bank(("yrow", half))
                    act.activation(yrow[:, 512 * half:512 * half + 512], bank[:, :], ACT.Identity).then_inc(by_act, 1)
                act.wait_ge(filled, pair_nth(p, ("spread",)))
                bank = pair_bank(("spread",))
                act.activation(ohT, bank[:, :], ACT.Identity).then_inc(by_act, 1)
            act.wait_ge(by_dve, led.total["dve"] + PAIRS * mcount["dve"])
            for i in range(TT):
                act.activation(cut(w28, TT, D)[:, i, :], H[:, i, :], ACT.Square, accum_out=ss[:, i:i + 1]
                               ).then_inc(squares, 1)
            square_root()

        @block.vector
        def _(dve):
            steps = [0]

            def step(ins):
                steps[0] += 1
                ins.then_inc(dve_step, 1)
                dve.wait_ge(dve_step, steps[0])

            def drain_groups(tag, dst, gain):
                for k in range(1, KT, 2):
                    dve.wait_ge(filled, nth((tag, k)))
                    bank = led.bank((tag, k))
                    if gain is None:
                        ins = dve.tensor_copy(dst[:, k, :], bank[:, :])
                    else:
                        ins = dve.tensor_scalar(dst[:, k, :], bank[:, :], gain[:, k:k + 1], None, ALU.mult)
                    ins.then_inc(by_dve, 1)

            roots = [0]

            def finish_root(c):
                roots[0] += 1
                dve.wait_ge(root_out, roots[0])
                r, m, t = rstd[:, 0:c], mean[:, 0:c], root[:, 0:c]
                step(dve.reciprocal(r, t))
                step(dve.tensor_tensor(t, r, r, ALU.mult))
                step(dve.tensor_tensor(t, t, m, ALU.mult))
                step(dve.tensor_scalar(t, t, -0.5, 1.5, ALU.mult, ALU.add))
                step(dve.tensor_tensor(r, r, t, ALU.mult))

            def inverse_root(n, widths=((0, 4, D),)):
                dve.wait_ge(squares, n)
                for c0, c1, w in widths[:-1]:
                    dve.tensor_scalar(mean[:, c0:c1], ss[:, c0:c1], 1.0 / w, EPS, ALU.mult, ALU.add)
                c0, c1, w = widths[-1]
                dve.tensor_scalar(mean[:, c0:c1], ss[:, c0:c1], 1.0 / w, EPS, ALU.mult, ALU.add
                                  ).then_inc(mean_ready, 1)
                c1 = widths[-1][1]
                finish_root(c1)

            def scale_rows(dst, src):
                for i in range(TT):
                    dve.tensor_scalar(dst[:, i, :], src[:, i, :], rstd[:, i:i + 1], None, ALU.mult
                                      ).then_inc(scaled, 1)

            def copy(dst, name, src=None):
                dve.wait_ge(filled, nth(name))
                bank = led.bank(name)
                dve.tensor_copy(dst, bank[:, :] if src is None else src(bank)).then_inc(by_dve, 1)

            def two_heads(dst, name, m):
                dve.wait_ge(filled, nth(name))
                bank = led.bank(name)
                dve.tensor_copy(dst[0:AD, 2 * m, :], bank[0:AD, :])
                dve.tensor_copy(dst[0:AD, 2 * m + 1, :], bank[AD:P, :]).then_inc(by_dve, 1)

            def shifted_scores(n, name, dsts, adds, scale):
                o = 4 * (n % 2)
                for i in range(TT):
                    dve.wait_ge(filled, nth((name[0], name[1], i)))
                    bank = led.bank((name[0], name[1], i))
                    w = dsts[i].shape[-1]
                    ins = dve.tensor_tensor_reduce(dsts[i], bank[:, 0:w], adds[i], scale, NEG, ALU.add, ALU.max,
                                                   mx[:, o + i:o + i + 1])
                    ins.then_inc(by_dve, 1)
                dve.wait_ge(*drained((name[0], name[1], 3)))
                if n >= 2:
                    dve.wait_ge(probs_in, 4 * (n - 1))
                dve.tensor_scalar(nmx[:, o:o + 4], mx[:, o:o + 4], -1.0, None, ALU.mult).then_inc(scores_in, 1)

            def row_inverses(n, last):
                if last is not None:
                    dve.wait_ge(*drained(last))
                dve.wait_ge(probs_in, 4 * n + 4)
                step(dve.reciprocal(rinv[:, 0:4], rs[:, 4 * (n % 2):4 * (n % 2) + 4]))

            Y_SCALED = [0]

            def tail(layer, mixT, y, hT, gate, sq):
                drain_groups(("mixed", layer), mixT, None)
                for half in range(2):
                    for i in range(TT):
                        copy(y[:, i, 512 * half:512 * half + 512], (("out", layer), half, i))
                inverse_root(sq)
                dve.wait_ge(dma_row, 16 * (layer + 1))
                for i in range(TT):
                    dve.scalar_tensor_tensor(y[:, i, :], y[:, i, :], rstd[:, i:i + 1], row[:, :], ALU.mult, ALU.mult
                                             ).then_inc(y_scaled, 1)
                for i in range(TT):
                    dve.wait_ge(y_scaled, 4 * layer + i + 1)
                    dve.tensor_tensor(H[:, i, :], H[:, i, :], y[:, i, :], ALU.add).then_inc(h_ready, 1)
                drain_groups(("h", layer), hT, None)
                for half in range(2):
                    for i in range(TT):
                        c = slice(512 * half, 512 * half + 512)
                        dve.wait_ge(*drained((("gate", layer), half, i)))
                        dve.wait_ge(filled, nth((("ple", layer), half, i)))
                        bank = led.bank((("ple", layer), half, i))
                        dve.tensor_tensor(gate[:, i, c], bank[:, :], gate[:, i, c], ALU.mult).then_inc(by_dve, 1)
                        dve.wait_ge(*drained((("ple", layer), half, i)))
                        dve.tensor_tensor(H[:, i, c], H[:, i, c], gate[:, i, c], ALU.add).then_inc(h_ready, 1)

            dve.wait_ge(tab_loaded, 64)
            dve.wait_ge(x_loaded, 16)
            inverse_root(4)
            scale_rows(U0, H)
            drain_groups("u0", UT, gain_u[0])
            dve.wait_ge(filled, nth(("forget",)))
            bank = led.bank(("forget",))
            dve.tensor_scalar(logf0[0], bank[0:AH, :], bf[0:AH, 0:1], None, ALU.add).then_inc(by_dve, 1)
            dve.wait_ge(*drained(("forget",)))
            dve.scalar_tensor_tensor(logf0[1], logf0[0], -1.0, logf0[0], ALU.mult, ALU.min).then_inc(logs, 1)
            dve.wait_ge(forget_logs, 2)
            step(dve.scalar_tensor_tensor(logf0[2], logf0[0], 0.0, logf0[1], ALU.min, ALU.subtract))
            step(dve.memset(logf0[0], 1.0))
            step(dve.tensor_tensor_scan(logf0[1], logf0[0], logf0[2], 0.0, ALU.mult, ALU.add))
            dve.tensor_scalar(logf0[3], logf0[1], -(AD ** 0.5), None, ALU.mult).then_inc(negc_ready, 1)
            for m in range(8):
                two_heads(k0, ("k0", m), m)
            for half in range(2):
                for i in range(1, TT, 2):
                    copy(v0[:, i, 512 * half:512 * half + 512], ("v0", half, i))
            dve.wait_ge(filled, nth(("g0", 1, 3)))
            for h in range(AH + 1):
                if h < AH:
                    if h >= 2:
                        dve.wait_ge(filled, nth(("o0", h - 2)))
                    shifted_scores(h, ("s0", h), [cut(prob0[h % 2] + tri[i], P * (i + 1)) for i in range(TT)],
                                   [causal[:, T - P * (i + 1):T] for i in range(TT)], AD ** -0.5)
                if h >= 1:
                    g = h - 1
                    if g == 0:
                        dve.wait_ge(*drained(("g0", 1, 3)))
                    row_inverses(g, ("o0", g - 1) if g else None)
                    dve.wait_ge(filled, nth(("o0", g)))
                    bank = led.bank(("o0", g))
                    for i in range(TT):
                        ins = dve.scalar_tensor_tensor(
                            g0[:, i, AD * g:AD * g + AD], bank[:, AD * i:AD * i + AD], rinv[:, i:i + 1],
                            g0[:, i, AD * g:AD * g + AD], ALU.mult, ALU.mult)
                    ins.then_inc(by_dve, 1)
            tail(0, mixT0, y0, hT0, gate0, 8)

            inverse_root(12)
            scale_rows(U1, H)
            drain_groups("u1", UT, gain_u[1])
            dve.tensor_tensor(lw[0], lb1, lb0, ALU.subtract).then_inc(lb_dve, 1)
            dve.wait_ge(lb_dve, 1)
            dve.scalar_tensor_tensor(lw[1], lw[0], -1.0, lw[0], ALU.mult, ALU.min).then_inc(lb_dve, 1)
            dve.wait_ge(lb_act, 2)
            dve.wait_ge(lb_dve, 2)
            step(dve.scalar_tensor_tensor(lw[4], lw[0], 0.0, lw[2], ALU.min, ALU.subtract))
            step(dve.tensor_scalar(lw[1], lw[0], -1.0, None, ALU.mult))
            step(dve.scalar_tensor_tensor(lw[3], lw[1], 0.0, lw[2], ALU.min, ALU.subtract))
            step(dve.tensor_tensor(lw[0], lw[3], lw[4], ALU.subtract))
            for h in range(RH):
                w = fwork[h % 2]
                hc = slice(h, h + 1)
                if h >= 2:
                    dve.wait_ge(f_act, 6 * (h - 2) + 6)
                dve.wait_ge(filled, nth(("f1", h)))
                bank = led.bank(("f1", h))
                dve.tensor_copy(w[0], bank[:, :]).then_inc(by_dve, 1)
                dve.wait_ge(*drained(("f1", h)))
                dve.scalar_tensor_tensor(w[1], w[0], -1.0, w[0], ALU.mult, ALU.min).then_inc(f_dve, 1)
                dve.wait_ge(f_act, 6 * h + 2)
                dve.scalar_tensor_tensor(w[2], w[0], 0.0, w[1], ALU.min, ALU.subtract).then_inc(f_dve, 1)
                dve.wait_ge(f_dve, 4 * h + 2)
                dve.tensor_tensor(w[3], w[2], w[0], ALU.subtract).then_inc(f_dve, 1)
                step(dve.tensor_scalar(w[5], w[2], lw[3][:, hc], lw[4][:, hc], ALU.add, ALU.max))
                dve.wait_ge(f_act, 6 * h + 6)
                step(dve.tensor_tensor(w[5], w[5], w[4], ALU.add))
                dve.tensor_tensor_scan(b1[:, h, :], reset, w[5], 0.0, ALU.mult, ALU.add).then_inc(f_dve, 1)
            dve.wait_ge(*drained(("g1", 1, 3)))
            for i in range(TT):
                gv = g1[:, i, :].rearrange("p (h v) -> p h v", h=RH)
                dve.tensor_tensor(gv, gv, rgain[:, None, :].broadcast_to([P, RH, P]), ALU.mult
                                  ).then_inc(g_scaled, 1)
            dve.wait_ge(f_dve, 4 * RH)
            def exponents(h):
                e = expo[h % 2]
                if h >= 2:
                    dve.wait_ge(filled, nth(("level", h - 2, LEVELS - 1)))
                for level in range(LEVELS):
                    half = 1 << level
                    ev = e[:, level, :].rearrange("p (n g s) -> p n g s", g=2, s=half)
                    bv = b1[:, h, :].rearrange("p (n g s) -> p n g s", g=2, s=half)
                    mid = bv[:, :, 0, half - 1:half].broadcast_to([P, T // (2 * half), half])
                    dve.tensor_tensor(ev[:, :, 1, :], bv[:, :, 1, :], mid, ALU.subtract)
                    ins = dve.tensor_tensor(ev[:, :, 0, :], mid, bv[:, :, 0, :], ALU.subtract)
                ins.then_inc(expo_in, 1)

            def chunk_exponents(h):
                if h >= 1:
                    dve.wait_ge(filled, nth(("kw", h - 1)))
                bc = b1[:, h, 0:384].rearrange("p (c t) -> p c t", c=3)
                dve.tensor_tensor(kd1[:, 0:384].rearrange("p (c t) -> p c t", c=3),
                                  bc[:, :, P - 1:P].broadcast_to([P, 3, P]), bc, ALU.subtract
                                  ).then_inc(last_in, 1)

            exponents(0)
            chunk_exponents(0)
            for h in range(RH):
                if h + 1 < RH:
                    exponents(h + 1)
                sT = sT1[h % 2]
                dve.wait_ge(filled, nth(("diag", h)))
                bank = led.bank(("diag", h))
                dve.tensor_tensor(sT, bank[:, :].rearrange("p (c t) -> p c t", c=TT),
                                            ident[:, None, :].broadcast_to([P, TT, P]), ALU.mult).then_inc(by_dve, 1)
                for level in range(LEVELS):
                    dve.wait_ge(*drained(("level", h, level - 1) if level else ("diag", h)))
                    half = 1 << level
                    n = 64 // half
                    dve.wait_ge(filled, nth(("level", h, level)))
                    bank = led.bank(("level", h, level))
                    src = bank[:, 0:256].rearrange("p (c n s) -> p c n s", c=TT, n=n)
                    dst = sT.rearrange("p c (n g s) -> p c n g s", g=2, s=half)[:, :, :, 1, :]
                    mk = maskt[:, 64 * level:64 * level + 64].rearrange("p (n s) -> p n s", n=n)
                    mk = mk[:, None].broadcast_to([P, TT, n, half])
                    dve.copy_predicated(dst, mk, src).then_inc(by_dve, 1)
                dve.wait_ge(last_done, 3 * h + 2)
                for c in range(TT - 1):
                    dve.wait_ge(filled, nth(("state", h, c)))
                    bank = led.bank(("state", h, c))
                    if c == 0:
                        dve.tensor_copy(st1[:, 0, :], bank[:, 0:P]).then_inc(by_dve, 1)
                    else:
                        dve.wait_ge(*drained(("state", h, c - 1)))
                        dve.scalar_tensor_tensor(st1[:, c, :], st1[:, c - 1, :], eb1[:, c:c + 1],
                                                           bank[:, 0:P], ALU.mult, ALU.add).then_inc(by_dve, 1)
                if h + 1 < RH:
                    chunk_exponents(h + 1)
                if h >= 1:
                    dve.wait_ge(gated, 4 * h)
                copy(oraw1[:, :, :], ("o1", h), src=lambda b: b[:, :].rearrange("p (c t) -> p c t", c=TT))
                dve.wait_ge(o_sq, 4 * h + 4)
                dve.tensor_scalar(mean[:, 0:4], ss[:, 0:4], 1.0 / P, EPS, ALU.mult, ALU.add
                                  ).then_inc(mean_ready, 1)
                finish_root(4)
                dve.wait_ge(g_scaled, 4)
                for i in range(TT):
                    gs = g1[:, i, P * h:P * h + P]
                    dve.scalar_tensor_tensor(gs, oraw1[:, i, :], rstd[:, i:i + 1], gs, ALU.mult, ALU.mult
                                             ).then_inc(gated, 1)
            tail(1, mixT1, y1, hT1, gate1, 16)

            inverse_root(20)
            scale_rows(U2, H)
            drain_groups("u2", UT, gain_u[2])

            def sine_argument(name, b, n):
                dve.wait_ge(misc, 96)
                dve.wait_ge(filled, nth(("u2", 7)))
                dve.wait_ge(filled, nth(name))
                bank = led.bank(name)
                x, r = fwork2[0], fwork2[1]
                dve.tensor_scalar(x, bank[0:64, :], fpar[0:64, b:b + 1], fpar[0:64, 2:3], ALU.add, ALU.mult).then_inc(by_dve, 1)
                dve.wait_ge(*drained(name))
                step(dve.tensor_scalar(r, x, 1.0 / (2.0 * np.pi), MAGIC, ALU.mult, ALU.add))
                step(dve.tensor_scalar(r, r, MAGIC, None, ALU.subtract))
                step(dve.scalar_tensor_tensor(x, r, -TWO_PI_HI, x, ALU.mult, ALU.add))
                step(dve.scalar_tensor_tensor(x, r, -TWO_PI_LO, x, ALU.mult, ALU.add))
                dve.tensor_scalar(x, x, PI_IN, -PI_IN, ALU.min, ALU.max).then_inc(sin_in, 1)

            sine_argument(("fh1",), 0, 1)
            dve.wait_ge(sin_out, 1)
            sine_argument(("fh2",), 1, 2)
            for m in range(4):
                two_heads(k2, ("k2", m), m)

            def taps(m, dst, tmp):
                step(dve.tensor_scalar(tmp, hy[:, m, 0:T], hyw[0][:, m:m + 1], hyw[3][:, m:m + 1], ALU.mult, ALU.add))
                step(dve.scalar_tensor_tensor(tmp, hy[:, m, 1:T + 1], hyw[1][:, m:m + 1], tmp, ALU.mult, ALU.add))
                step(dve.scalar_tensor_tensor(dst, hy[:, m, 2:T + 2], hyw[2][:, m:m + 1], tmp, ALU.mult, ALU.add))

            dve.wait_ge(*drained(("hy", 5)))
            for m in range(2):
                taps(2 + m, tmpA, tmpA)
                taps(4 + m, tmpB, tmpB)
                dve.tensor_tensor(hy[:, 2 + m, 0:T], tmpA, tmpB, ALU.mult).then_inc(z_ready, 1)
                dve.wait_ge(z_ready, m + 1)
            for m in range(2):
                taps(m, hy[:, 4 + m, 0:T], tmpA)
            dve.wait_ge(*drained(("pool", 1)))
            dve.wait_ge(decay_loaded, 32)
            step(dve.memset(psum_t[:, :, 0:9], 0.0))
            for m in range(2):
                step(dve.memset(tmpB, 1.0))
                step(dve.tensor_tensor_scan(psum_t[:, m, 9:T + 9], tmpB, praw[:, m, :], 0.0, ALU.mult, ALU.add))
                step(dve.tensor_copy(psum_t[:, m, T + 9:T + 16],
                                     psum_t[:, m, T + 8:T + 9].broadcast_to([P, 7])))
            for g, w in enumerate((2, 4, 8, 16)):
                m, r0 = g // 2, 64 * (g % 2)
                rr = slice(r0, r0 + 64)
                hw = w // 2
                step(dve.tensor_tensor(pdiff[rr, m, :], psum_t[rr, m, 8 + hw:8 + hw + T],
                                       psum_t[rr, m, 8 - hw:8 - hw + T], ALU.subtract))
                step(dve.tensor_tensor(pdiff[rr, m, :], pdiff[rr, m, :], invc[rr, m, :], ALU.mult))
                dve.tensor_tensor(pdiff[rr, m, :], pdiff[rr, m, :], praw[rr, m, :], ALU.subtract
                                  ).then_inc(pool_ready, 1)
            for i in range(TT):
                dve.wait_ge(filled, nth(("fh3", i)))
                bank = led.bank(("fh3", i))
                dve.tensor_tensor(fh[:, i, :], bank[:, :], decay[:, i, :], ALU.mult).then_inc(by_dve, 1)
            dve.wait_ge(*drained(("fh3", 3)))
            for i in range(TT):
                tmp = tmpA[:, 0:256] if i % 2 == 0 else tmpB[:, 0:256]
                step(dve.tensor_tensor(tmp, fh[:, i, 0:256], fh[:, i, 256:512], ALU.subtract))
                step(dve.tensor_tensor(fh[:, i, 0:256], fh[:, i, 0:256], fh[:, i, 256:512], ALU.add))
                dve.tensor_copy(fh[:, i, 256:512], tmp).then_inc(fsum, 1)
            dve.wait_ge(fsum, 4)
            dve.wait_ge(*drained(("H", 3)))
            dve.wait_ge(*drained(("Z", 3)))
            zr, zi, hr, hi = fh[:, :, 0:256], fh[:, :, 256:512], hs[:, :, 0:256], hs[:, :, 256:512]
            step(dve.tensor_tensor(zrow, zr, hr, ALU.mult))
            step(dve.tensor_tensor(tmp2, zi, hi, ALU.mult))
            step(dve.tensor_tensor(zrow, zrow, tmp2, ALU.subtract))
            step(dve.tensor_tensor(tmp2, zr, hi, ALU.mult))
            step(dve.tensor_tensor(zi, zi, hr, ALU.mult))
            dve.tensor_tensor(tmp2, tmp2, zi, ALU.add).then_inc(prod_ready, 1)
            dve.wait_ge(pool_ready, 4)
            for i in range(TT):
                dve.wait_ge(filled, nth(("pooled", i)))
                bank = led.bank(("pooled", i))
                dve.tensor_tensor(mix[:, i, 768:1024], bank[:, 0:256], pscale[:, :], ALU.mult).then_inc(by_dve, 1)
            for m in range(2):
                dve.wait_ge(filled, nth(("conv", m)))
                bank = led.bank(("conv", m))
                dve.scalar_tensor_tensor(hy[:, m, 0:T], hy[:, 2 + m, 0:T], skip[:, m:m + 1], bank[:, :],
                                                   ALU.mult, ALU.add).then_inc(by_dve, 1)
                dve.wait_ge(*drained(("conv", m)))
                dve.tensor_tensor(hy[:, m, 0:T], hy[:, m, 0:T], hy[:, 4 + m, 0:T], ALU.mult).then_inc(yh_ready, 1)
            for h in range(NH + 1):
                if h < NH:
                    if h >= 2:
                        dve.wait_ge(filled, nth(("o2", h - 2)))
                    else:
                        dve.wait_ge(filled, nth(("pooled", 3)))
                    bb = bias2[h % 2]
                    dve.wait_ge(h_bias[h % 2], 32 * (h // 2 + 1))
                    step(dve.tensor_tensor(bb, raw2[h % 2][:, :, ::-1], window[:, None, :].broadcast_to([P, 14, GW]), ALU.add))
                    shifted_scores(AH + h, ("s2", h), [cut(prob2[h % 2] + T * i, T) for i in range(TT)],
                                   [bb[:, 6 - 2 * i:14 - 2 * i, :].rearrange("p a b -> p (a b)") for i in range(TT)],
                                   1.0)
                if h >= 1:
                    g = h - 1
                    row_inverses(AH + g, ("o2", g - 1) if g else None)
                    dve.wait_ge(filled, nth(("o2", g)))
                    bank = led.bank(("o2", g))
                    for i in range(TT):
                        c = 256 + AD * g
                        ins = dve.tensor_scalar(mix[:, i, c:c + AD], bank[:, AD * i:AD * i + AD], rinv[:, i:i + 1],
                                                None, ALU.mult)
                    ins.then_inc(by_dve, 1)
            inverse_root(32, ((0, 4, 256), (4, 8, 512), (8, 12, 256)))
            for i in range(TT):
                for n, (c0, c1) in enumerate(((0, 256), (256, 768), (768, 1024))):
                    ins = dve.tensor_scalar(mix[:, i, c0:c1], mix[:, i, c0:c1], rstd[:, 4 * n + i:4 * n + i + 1], None,
                                            ALU.mult)
                ins.then_inc(mixed_ready, 1)
            drain_groups("mix", mixT2, gain_mix)
            for half in range(2):
                for i in range(TT):
                    c = slice(512 * half, 512 * half + 512)
                    dve.wait_ge(filled, nth(("out2", half, i)))
                    bank = led.bank(("out2", half, i))
                    dve.tensor_tensor(H[:, i, c], H[:, i, c], bank[:, :], ALU.add).then_inc(by_dve, 1)
            inverse_root(36)
            dve.wait_ge(*drained(("out2", 1, 3)))
            scale_rows(hn, H)
            drain_groups("u3", hnT, gain_u[3])
            dve.wait_ge(filled, nth(("router",)))
            bank = led.bank(("router",))
            av = aff.rearrange("p (i e) -> p i e", i=TT)
            dve.tensor_copy(aff, bank[:, 0:64]).then_inc(by_dve, 1)
            dve.wait_ge(*drained(("router",)))
            step(dve.tensor_reduce(rmax, av, AX, ALU.max))
            dve.tensor_tensor(av, av, rmax[:, :, None].broadcast_to([P, TT, NE]), ALU.subtract).then_inc(rt_in, 1)
            dve.wait_ge(rt_exp, 1)
            step(dve.tensor_reduce(rsumr, av, AX, ALU.add))
            step(dve.reciprocal(rsumr, rsumr))
            dve.tensor_tensor(av, av, rsumr[:, :, None].broadcast_to([P, TT, NE]), ALU.mult).then_inc(rt_out, 1)
            dve.wait_ge(rt_out, 1)
            copy(affT, ("aff",), src=lambda b: b[0:NE, :])
            dve.wait_ge(*drained(("aff",)))
            for r in range(CAP // 8):
                step(dve.max(top8, affT))
                step(dve.match_replace(affT, top8, affT, -1.0))
            step(dve.tensor_scalar(selT, affT, 0.0, None, ALU.is_lt))
            step(dve.memset(scratchT, 1.0))
            step(dve.tensor_tensor_scan(posT, scratchT, selT, 0.0, ALU.mult, ALU.add))
            dve.tensor_tensor(posT, posT, selT, ALU.mult).then_inc(loop_ready, 1)
            copy(pos, ("slot",), src=lambda b: b[:, 0:64])
            dve.wait_ge(*drained(("slot",)))
            for i in range(TT):
                pv = pos[:, NE * i:NE * i + NE]
                dve.tensor_tensor(onehot[:, i, :, :], pv[:, :, None].broadcast_to([P, NE, CAP]),
                                  slots[:, None, :].broadcast_to([P, NE, CAP]), ALU.is_equal
                                  ).then_inc(loop_ready, 1)
            dve.wait_ge(loop_ready, 5)

            with dve.Fori(0, PAIRS) as p:
                ohv = onehot.rearrange("p i e s -> p i (e s)")
                for i in range(TT):
                    ins = dve.tensor_copy(ohp[:, i, :], ohv[:, i, bass.ds(p * P, P)])
                ins.then_inc(pair_oh, 1)
                for i in range(TT):
                    for e in range(2):
                        g = small[:, bass.ds(p * 2 + (96 + NE * i + e), 1)].broadcast_to([P, CAP])
                        ins = dve.tensor_tensor(gop[:, i, CAP * e:CAP * e + CAP],
                                                ohv[:, i, bass.ds(p * P + CAP * e, CAP)], g, ALU.mult)
                ins.then_inc(pair_oh, 1)
                for half in range(2):
                    dve.wait_ge(filled, pair_nth(p, ("xs", half)))
                    bank = pair_bank(("xs", half))
                    dve.tensor_tensor(xs[:, 4 * half:4 * half + 4, :],
                                              bank[:, :].rearrange("p (k s) -> p k s", k=4),
                                              gain_u[3][:, 4 * half:4 * half + 4][:, :, None].broadcast_to([P, 4, P]),
                                              ALU.mult).then_inc(by_dve, 1)
                for e in range(2):
                    for f in range(4):
                        dve.wait_ge(*pair_drained(p, ("gate", e, f)))
                        dve.wait_ge(filled, pair_nth(p, ("up", e, f)))
                        bank = pair_bank(("up", e, f))
                        dve.tensor_tensor(hT[e][:, 4 * f:4 * f + 4, :],
                                                  bank[:, 0:256].rearrange("p (m s) -> p m s", m=4),
                                                  act_t[f % 2].rearrange("p (m s) -> p m s", m=4), ALU.mult).then_inc(by_dve, 1)
                for half in range(2):
                    for i in range(TT):
                        c = slice(512 * half, 512 * half + 512)
                        dve.wait_ge(filled, pair_nth(p, ("add", half, i)))
                        bank = pair_bank(("add", half, i))
                        dve.tensor_tensor(H[:, i, c], H[:, i, c], bank[:, :], ALU.add).then_inc(by_dve, 1)
            dve.wait_ge(by_dve, led.total["dve"] + PAIRS * mcount["dve"])
            inverse_root(40)
            dve.wait_ge(dma_row, 48)
            for i in range(TT):
                dve.scalar_tensor_tensor(cut(w28, TT, D)[:, i, :], H[:, i, :], rstd[:, i:i + 1], row[:, :],
                                         ALU.mult, ALU.mult).then_inc(final_in, 1)


INPUTS = ["x", "p", "norm_post", "att_w_in", "att_b_f", "att_w_out", "rec_w_in", "rec_out_norm", "rec_w_out",
          "ple_w_proj", "ple_w_gate", "w_in_2", "hy_f_w1_2", "hy_f_w2_2", "hy_f_wout_2", "na_rpb_2", "pool_w_2",
          "pool_scale_2", "w_out_2", "w_router_2", "w_gate_2", "w_up_2", "w_down_2", "final_g_2"]


def kernel(**inputs):
    import concourse.bacc as bacc
    from concourse.bass_utils import run_bass_kernel_spmd

    v = {n: np.asarray(x) for n, x in inputs.items()}
    column = lambda x: x.reshape(-1, P).T
    arrays = {n: v[n] for n in INPUTS}
    arrays["x"] = v["x"][0]
    arrays["p"] = v["p"][:, 0].transpose(0, 2, 1)
    for n in ("att_w_in", "att_w_out", "rec_w_in", "rec_w_out", "w_in_2", "hy_f_w1_2", "hy_f_w2_2",
              "hy_f_wout_2", "pool_w_2", "w_out_2", "w_router_2", "w_gate_2", "w_up_2", "w_down_2", "rec_out_norm",
              "pool_scale_2"):
        arrays[n] = v[n][0]
    arrays["att_b_f"] = v["att_b_f"].reshape(AH, 1)
    arrays["na_rpb_2"] = v["na_rpb_2"][..., ::-1].reshape(-1)
    arrays["filter_params"] = np.stack([v["hy_f_b1_2"][0], v["hy_f_b2_2"][0], v["hy_f_freq_2"][0]], axis=1)
    taps = v["hy_short_w_2"][0]
    parts = [v["norm_pre"][0], v["norm_pre"][1], v["norm1_g_2"][0], v["norm2_g_2"][0], v["mix_norm_g_2"][0],
             taps[0], taps[1], taps[2], v["hy_short_b_2"][0], v["hy_skip_2"][0], v["rec_lb"][0], v["rec_lb"][1]]
    packed = np.zeros((P, 90), np.float32)
    packed[:, 0:82] = np.concatenate([column(x) for x in parts], axis=1)
    arrays["cols"] = packed
    arrays.update(constants())

    nc = bacc.Bacc("TRN2", target_bir_lowering=False, num_devices=1)
    given, a = {}, {}
    for name, x in arrays.items():
        given[f"in_{name}"] = np.ascontiguousarray(x)
        a[name] = nc.dram_tensor(f"in_{name}", x.shape, mybir.dt.from_np(x.dtype), kind="ExternalInput").ap()
    a["rpb_padded"] = nc.dram_tensor("rpb_padded", (NH * RPB_ROWS * RPB_COLS + 128,), F32, kind="Internal").ap()
    out = nc.dram_tensor("out", (T, D), F32, kind="ExternalOutput").ap()
    two_blocks(nc, a, out)
    r = run_bass_kernel_spmd(nc, [given], core_ids=[0])
    return r.results[0]["out"].reshape(1, T, D)
```
